# Optimizing a Trainium2 kernel written in Bass

```python
import math
import jax
import jax.numpy as jnp
from jax import lax
import numpy as np

D_MODEL = 1024
BATCH = 1
SEQ = 128
DEPTH = 2
DEC_BATCH = 1
DEC_SEQ = 256
PAST_LEN = 128

GRID_W = 64
N_HEADS = 4
GLA_DK = 64
GLA_DV = 128
GLA_RANK = 16
GLA_TEMP = 16.0
GLA_CHUNK = 64
CONV_CH = 512
CONV_WIDTH = 31
CONV_PAD = (CONV_WIDTH - 1) // 2
DIFF_DH = 64
DIFF_DV = 128
ROPE_FREQS = DIFF_DH // 4
ROPE_BASE = 10000.0
Q_BLOCK = 128
FFN_HIDDEN = -(-8 * D_MODEL // (3 * 256)) * 256
EPS = 1e-6
N_BRANCH = 3

GLA_QW = N_HEADS * GLA_DK
GLA_VW = N_HEADS * GLA_DV
DIFF_QW = N_HEADS * 2 * DIFF_DH
DIFF_VW = N_HEADS * DIFF_DV
SPLITS = (GLA_QW, GLA_QW, GLA_VW, GLA_VW, 2 * GLA_RANK, 2 * CONV_CH, DIFF_QW, DIFF_QW, DIFF_VW, N_BRANCH * D_MODEL)
SPLIT_IDX = tuple(sum(SPLITS[:i + 1]) for i in range(len(SPLITS) - 1))
IN_WIDTH = sum(SPLITS)
BRANCH_WIDTHS = (GLA_VW, CONV_CH, DIFF_VW)
BRANCH_TOTAL = sum(BRANCH_WIDTHS)

kernel_name = 'hybrid_gla_conformer_diffattn_dit_step'

F32 = jnp.float32

def rmsnorm(x, g):
    xf = x.astype(F32)
    y = xf * lax.rsqrt(jnp.mean(xf * xf, axis=-1, keepdims=True) + EPS)
    return (y * g.astype(F32)).astype(x.dtype)

def layernorm(x, g, b):
    xf = x.astype(F32)
    mu = jnp.mean(xf, axis=-1, keepdims=True)
    var = jnp.mean(jnp.square(xf - mu), axis=-1, keepdims=True)
    y = (xf - mu) * lax.rsqrt(var + EPS)
    return (y * g.astype(F32) + b.astype(F32)).astype(x.dtype)

def axial_rope(n_tokens):
    rows = n_tokens // GRID_W
    row = jnp.repeat(jnp.arange(rows, dtype=F32), GRID_W)
    col = jnp.tile(jnp.arange(GRID_W, dtype=F32), rows)
    inv = ROPE_BASE ** (-jnp.arange(ROPE_FREQS, dtype=F32) / ROPE_FREQS)
    ang = jnp.stack([row[:, None] * inv, col[:, None] * inv], axis=1)
    return jnp.cos(ang), jnp.sin(ang)

def apply_rope(x, cos, sin):
    shp = x.shape
    xr = x.reshape(shp[:-1] + (2, 2, ROPE_FREQS)).astype(F32)
    x1, x2 = xr[..., 0, :], xr[..., 1, :]
    c = cos[:, None, None]
    s = sin[:, None, None]
    out = jnp.stack([x1 * c - x2 * s, x1 * s + x2 * c], axis=-2)
    return out.reshape(shp).astype(x.dtype)

def gla_chunk_scan(q, k, v, log_a, s0):
    B, L, H, _ = q.shape
    n = L // GLA_CHUNK

    def chunks(t):
        return jnp.moveaxis(t.astype(F32).reshape((B, n, GLA_CHUNK) + t.shape[2:]), 1, 0)

    mask = jnp.tril(jnp.ones((GLA_CHUNK, GLA_CHUNK), dtype=bool))[None, :, :, None, None]

    def step(s, inp):
        qc, kc, vc, gc = inp
        b = jnp.cumsum(gc, axis=1)
        inter = jnp.einsum('bchk,bhkv->bchv', qc * jnp.exp(b), s)
        rel = jnp.where(mask, b[:, :, None] - b[:, None, :], -jnp.inf)
        attn = jnp.einsum('bihk,bjhk,bijhk->bhij', qc, kc, jnp.exp(rel))
        intra = jnp.einsum('bhij,bjhv->bihv', attn, vc)
        b_last = b[:, -1]
        s_new = s * jnp.exp(b_last)[..., None] + jnp.einsum('bjhk,bjhv->bhkv', kc * jnp.exp(b_last[:, None] - b), vc)
        return s_new, inter + intra

    s_fin, o = lax.scan(step, s0, (chunks(q), chunks(k), chunks(v), chunks(log_a)))
    o = jnp.moveaxis(o, 0, 1).reshape(B, L, H, -1).astype(v.dtype)
    return o, s_fin

def gla_branch(q, k, v, g, lr, w_a2, b_a, norm_g, s0f, s0b):
    B, L, _ = q.shape
    q = q.reshape(B, L, N_HEADS, GLA_DK) * (GLA_DK ** -0.5)
    k = k.reshape(B, L, N_HEADS, GLA_DK)
    v = v.reshape(B, L, N_HEADS, GLA_DV)
    lr_f, lr_b = jnp.split(lr, 2, axis=-1)
    log_a_f = (jax.nn.log_sigmoid((lr_f @ w_a2[0] + b_a[0]).astype(F32)) / GLA_TEMP).reshape(B, L, N_HEADS, GLA_DK)
    log_a_b = (jax.nn.log_sigmoid((lr_b @ w_a2[1] + b_a[1]).astype(F32)) / GLA_TEMP).reshape(B, L, N_HEADS, GLA_DK)
    o_f, s_f = gla_chunk_scan(q, k, v, log_a_f, s0f)
    flip = lambda t: jnp.flip(t, axis=1)
    o_b, s_b = gla_chunk_scan(flip(q), flip(k), flip(v), flip(log_a_b), s0b)
    o = rmsnorm(o_f + flip(o_b), norm_g) * jax.nn.silu(g.reshape(B, L, N_HEADS, GLA_DV))
    return o.reshape(B, L, GLA_VW), s_f, s_b

def conv_branch(u, w, b, ln_g, ln_b):
    a, gate = jnp.split(u, 2, axis=-1)
    y = a * jax.nn.sigmoid(gate)
    y = lax.conv_general_dilated(y, w[:, None, :], window_strides=(1,), padding=[(CONV_PAD, CONV_PAD)],
                                 dimension_numbers=('NWC', 'WIO', 'NWC'), feature_group_count=CONV_CH) + b
    return jax.nn.silu(layernorm(y, ln_g, ln_b))

def diff_attention(q, k, v, lam):
    B, Lq = q.shape[:2]
    nq = Lq // Q_BLOCK
    qb = jnp.moveaxis(q.reshape((B, nq, Q_BLOCK) + q.shape[2:]), 1, 0)
    scale = DIFF_DH ** -0.5

    def block(qi):
        s = jnp.einsum('bqhtd,bkhtd->bhtqk', qi, k).astype(F32) * scale
        p = jax.nn.softmax(s, axis=-1)
        w = (p[:, :, 0] - lam * p[:, :, 1]).astype(v.dtype)
        return jnp.einsum('bhqk,bkhv->bqhv', w, v)

    o = lax.map(block, qb)
    return jnp.moveaxis(o, 0, 1).reshape(B, Lq, N_HEADS, DIFF_DV)

def trunk_layer(x, cond, l, lw, ctx, rope):
    B, L, _ = x.shape
    mod = (jax.nn.silu(cond) @ lw['w_mod'] + lw['b_mod'])[:, None, :]
    sh1, sc1, g1, sh2, sc2, g2 = jnp.split(mod, 6, axis=-1)
    h = rmsnorm(x, lw['norm1_g']) * (1.0 + sc1) + sh1
    proj = h @ lw['w_in']
    gq, gk, gv, gg, glr, cu, dq, dk, dv, gates = jnp.split(proj, SPLIT_IDX, axis=-1)

    if ctx is None:
        s0f = jnp.zeros((B, N_HEADS, GLA_DK, GLA_DV), F32)
        s0b = s0f
    else:
        s0f = ctx[2][:, 0].astype(F32)
        s0b = ctx[2][:, 1].astype(F32)
    o_gla, s_f, s_b = gla_branch(gq, gk, gv, gg, glr, lw['gla_w_a2'], lw['gla_b_a'], lw['gla_norm_g'], s0f, s0b)

    o_conv = conv_branch(cu, lw['conv_w'], lw['conv_b'], lw['conv_ln_g'], lw['conv_ln_b'])

    dq = dq.reshape(B, L, N_HEADS, 2, DIFF_DH)
    dk = dk.reshape(B, L, N_HEADS, 2, DIFF_DH)
    dv = dv.reshape(B, L, N_HEADS, DIFF_DV)
    lam_init = 0.8 - 0.6 * math.exp(-0.3 * l)
    lq1, lk1, lq2, lk2 = lw['diff_lambda'].astype(F32)
    lam = jnp.exp(jnp.sum(lq1 * lk1)) - jnp.exp(jnp.sum(lq2 * lk2)) + lam_init
    if ctx is None:
        keys, vals = dk, dv
    else:
        dq = apply_rope(dq, rope[0], rope[1])
        dk = apply_rope(dk, rope[0], rope[1])
        keys = jnp.concatenate([dk, ctx[0].astype(dk.dtype)], axis=1)
        vals = jnp.concatenate([dv, ctx[1].astype(dv.dtype)], axis=1)
    o_diff = diff_attention(dq, keys, vals, lam)
    o_diff = (rmsnorm(o_diff, lw['diff_subln_g']) * (1.0 - lam_init)).reshape(B, L, DIFF_VW)

    wb = lw['w_branch']
    ga, gb, gc = jnp.split(jax.nn.sigmoid(gates), N_BRANCH, axis=-1)
    o1 = BRANCH_WIDTHS[0]
    o2 = o1 + BRANCH_WIDTHS[1]
    merged = ga * (o_gla @ wb[:o1]) + gb * (o_conv @ wb[o1:o2]) + gc * (o_diff @ wb[o2:])
    x = x + g1 * (merged @ lw['w_out'])

    h2 = rmsnorm(x, lw['norm2_g']) * (1.0 + sc2) + sh2
    a, b = jnp.split(h2 @ lw['w_ffn_in'], 2, axis=-1)
    x = x + g2 * ((jax.nn.silu(a) * b) @ lw['w_ffn_out'])
    if ctx is None:
        return x, (dk, dv, jnp.stack([s_f, s_b], axis=1).astype(x.dtype))
    return x, None

def setup_inputs(seed: int = 0) -> dict:
    key = jax.random.key(seed)
    ks = jax.random.split(key, 32)
    nrm = lambda k, shape, s: jax.random.normal(k, shape, F32) * s
    ones = lambda k, shape: 1.0 + 0.05 * jax.random.normal(k, shape, F32)
    D = D_MODEL
    return {
        'x_prompt': nrm(ks[0], (BATCH, SEQ, D), 1.0),
        'x_sample': nrm(ks[1], (DEC_BATCH, DEC_SEQ, D), 1.0),
        'cache_diff_k': nrm(ks[2], (DEC_BATCH, DEPTH, PAST_LEN, N_HEADS, 2, DIFF_DH), 1.0),
        'cache_diff_v': nrm(ks[3], (DEC_BATCH, DEPTH, PAST_LEN, N_HEADS, DIFF_DV), 1.0),
        'state_gla': nrm(ks[4], (DEC_BATCH, DEPTH, 2, N_HEADS, GLA_DK, GLA_DV), 0.5),
        'c': nrm(ks[5], (DEC_BATCH, D), 1.0),
        'c_ctx': nrm(ks[6], (D,), 1.0),
        'w_mod': nrm(ks[7], (DEPTH, D, 6 * D), 0.5 * D ** -0.5),
        'b_mod': nrm(ks[8], (DEPTH, 6 * D), 0.02),
        'norm1_g': ones(ks[9], (DEPTH, D)),
        'norm2_g': ones(ks[10], (DEPTH, D)),
        'w_in': nrm(ks[11], (DEPTH, D, IN_WIDTH), D ** -0.5),
        'gla_w_a2': nrm(ks[12], (DEPTH, 2, GLA_RANK, GLA_QW), GLA_RANK ** -0.5),
        'gla_b_a': nrm(ks[13], (DEPTH, 2, GLA_QW), 0.1),
        'gla_norm_g': ones(ks[14], (DEPTH, GLA_DV)),
        'conv_w': nrm(ks[15], (DEPTH, CONV_WIDTH, CONV_CH), CONV_WIDTH ** -0.5),
        'conv_b': nrm(ks[16], (DEPTH, CONV_CH), 0.02),
        'conv_ln_g': ones(ks[17], (DEPTH, CONV_CH)),
        'conv_ln_b': nrm(ks[18], (DEPTH, CONV_CH), 0.02),
        'diff_lambda': nrm(ks[19], (DEPTH, 4, DIFF_DH), 0.1),
        'diff_subln_g': ones(ks[20], (DEPTH, DIFF_DV)),
        'w_branch': nrm(ks[21], (DEPTH, BRANCH_TOTAL, D), (BRANCH_TOTAL // N_BRANCH) ** -0.5),
        'w_out': nrm(ks[22], (DEPTH, D, D), D ** -0.5),
        'w_ffn_in': nrm(ks[23], (DEPTH, D, 2 * FFN_HIDDEN), D ** -0.5),
        'w_ffn_out': nrm(ks[24], (DEPTH, FFN_HIDDEN, D), FFN_HIDDEN ** -0.5),
        'final_norm_g': ones(ks[25], (D,)),
    }

def reference(x_prompt, x_sample, cache_diff_k, cache_diff_v, state_gla, c, c_ctx, w_mod, b_mod,
              norm1_g, norm2_g, w_in, gla_w_a2, gla_b_a, gla_norm_g, conv_w, conv_b, conv_ln_g,
              conv_ln_b, diff_lambda, diff_subln_g, w_branch, w_out, w_ffn_in, w_ffn_out, final_norm_g):
    rope = axial_rope(x_sample.shape[1])
    xp = x_prompt
    xs = x_sample
    new_k, new_v, new_s = [], [], []
    for l in range(DEPTH):
        lw = {
            'w_mod': w_mod[l], 'b_mod': b_mod[l], 'norm1_g': norm1_g[l], 'norm2_g': norm2_g[l],
            'w_in': w_in[l], 'gla_w_a2': gla_w_a2[l], 'gla_b_a': gla_b_a[l], 'gla_norm_g': gla_norm_g[l],
            'conv_w': conv_w[l], 'conv_b': conv_b[l], 'conv_ln_g': conv_ln_g[l], 'conv_ln_b': conv_ln_b[l],
            'diff_lambda': diff_lambda[l], 'diff_subln_g': diff_subln_g[l], 'w_branch': w_branch[l],
            'w_out': w_out[l], 'w_ffn_in': w_ffn_in[l], 'w_ffn_out': w_ffn_out[l],
        }
        xp, (k_l, v_l, s_l) = trunk_layer(xp, c_ctx[None, :], l, lw, None, None)
        new_k.append(k_l)
        new_v.append(v_l)
        new_s.append(s_l)
        xs, _ = trunk_layer(xs, c, l, lw, (cache_diff_k[:, l], cache_diff_v[:, l], state_gla[:, l]), rope)
    y_prompt = rmsnorm(xp, final_norm_g)
    y_sample = rmsnorm(xs, final_norm_g)
    new_diff_k = jnp.stack(new_k, axis=1)
    new_diff_v = jnp.stack(new_v, axis=1)
    new_state_gla = jnp.stack(new_s, axis=1)
    return (y_prompt, y_sample, new_diff_k, new_diff_v, new_state_gla)


_drawn_inputs = setup_inputs


def setup_inputs(seed=0):
    import zlib

    import numpy as np

    out = dict(_drawn_inputs(seed))
    spreads = {}
    factors = {'state_gla': 8.0,
     'norm2_g': 2.669,
     'gla_norm_g': 7.315,
     'conv_b': 8.0,
     'conv_ln_g': 6.431,
     'conv_ln_b': 23.707,
     'diff_lambda': 8.0,
     'diff_subln_g': 6.222}
    for name, (base, spread) in spreads.items():
        noise = np.random.default_rng([zlib.crc32(name.encode()), seed]).standard_normal(out[name].shape)
        drawn = base * np.exp(spread * noise) if base else spread * noise
        out[name] = jnp.asarray(drawn.astype(out[name].dtype))
    for name, factor in factors.items():
        out[name] = (out[name] * factor).astype(out[name].dtype)
    return out
```

```python
from contextlib import ExitStack
import math

import concourse.bass as bass
from concourse import mybir

F32 = mybir.dt.float32
F32R = mybir.dt.float32r
U8 = mybir.dt.uint8
ALU = mybir.AluOpType
ACT = mybir.ActivationFunctionType
AX_X = mybir.AxisListType.X

P = 128
D = 1024
KD = D // P
DEPTH = 2
TP, TS = 128, 256
T = TP + TS
NT = T // P
H = 4
DK = 64
DV = 128
RANK = 16
CONV = 512
CT = CONV // P
TAPS = 31
PAD = TAPS // 2
HID = 2816
KH = HID // P
EPS = 1e-6

C_GQ, C_GK, C_GV, C_GG, C_LR, C_CA, C_CG, C_DQ, C_DK, C_DV, C_GATE = (
    0, 256, 512, 1024, 1536, 1568, 2080, 2592, 3104, 3616, 4128)

YW = PAD + TP + PAD + TS + PAD
AW = TP + PAD + TS
Y_P, Y_S = PAD, PAD + TP + PAD
A_S = TP + PAD

RAW, SPL = 2, 4
IN_CHUNKS = ([(C_CA, 256), (C_CG, 256), (C_CA + 256, 256), (C_CG + 256, 256), (C_GG, 256), (C_GG + 256, 256),
              (C_LR, 2 * RANK), (C_GQ, 256), (C_GK, 256), (C_GV, 256), (C_GV + 256, 256),
              (C_DQ, 256), (C_DQ + 256, 256), (C_DK, 256), (C_DK + 256, 256), (C_DV, 256), (C_DV + 256, 256)]
             + [(C_GATE + 256 * i, 256) for i in range(12)])
N_IN = 2 * len(IN_CHUNKS)
N_BR = 12
N_WO = 8
PAIRS = KH // 2
N_FI = 4 * PAIRS
N_FO = KH
BR0, WO0, FI0, FO0 = N_IN, N_IN + N_BR, N_IN + N_BR + N_WO, N_IN + N_BR + N_WO + N_FI
PIECES = FO0 + N_FO
assert PIECES % SPL == 0 and PIECES % RAW == 0

MODR = 4
MOD_CHUNKS = 6 * D // 512
MOD_PE = 2
assert MOD_CHUNKS == PAIRS + 1

LEVELS = 7
ROUNDS = LEVELS + 2
UNITS = [(h, q) for h in range(H) for q in range(NT)]

LN_EXP = "natural_log_exp_and_others"

R_BMOD, R_N1, R_N2, R_BA, R_GN, R_CB, R_LG, R_LB, R_SUB, R_FN, R_END = (
    0, 48, 56, 64, 68, 69, 73, 77, 81, 82, 90)


class Signal:

    def __init__(self, nc, ctx, name, per=1, credit=0):
        self.sem = ctx.enter_context(nc.semaphore(name))
        self.per, self.credit, self.seen = per, credit, 0

    def at(self, layer, n):
        assert n + self.credit >= 1, n
        return self.sem, layer * self.per + (n + self.credit)

    def next(self):
        self.seen = self.seen % self.per + 1
        return self.seen


def memory(nc):
    m = {}
    top = [16512]

    def own(name, shape, dt=F32, size=None):
        n = size or math.prod(shape[1:]) * (1 if dt == U8 else 4)
        m[name] = nc.alloc_sbuf_tensor_at(name, shape, dt, offset=top[0])
        at = top[0]
        top[0] += (n + 31) // 32 * 32
        return at

    def over(name, shape, offset, dt=F32):
        m[name] = nc.alloc_sbuf_tensor_at(name, shape, dt, offset=offset)

    own("x", [P, KD, T])
    own("h_hi", [P, KD, T], F32R)
    own("h_lo", [P, KD, T], F32R)
    own("w_raw", [P, RAW, 1024])
    own("w_hi", [P, SPL, 1024], F32R)
    own("w_lo", [P, SPL, 1024], F32R)
    own("k_rows", [P, 512])
    gates = own("gates", [P, 24, T])
    gla = own("gla_hi", [P, H, T], F32R)
    own("gla_lo", [P, H, T], F32R)
    conv = own("conv_hi", [P, CT, T], F32R)
    conv_lo = own("conv_lo", [P, CT, T], F32R)
    diff = own("diff_hi", [P, H, T], F32R)
    diff_lo = own("diff_lo", [P, H, T], F32R)
    over("act_hi", [P, KH, T], gates, F32R)
    over("act_lo", [P, KH, T], gates + KH * T * 4, F32R)
    over("stage", [P, NT, D], gates)
    over("masks_in", [P, LEVELS, P], gates + NT * D * 4)
    over("conv_in", [P, CT, YW], gates + 15 * T * 4)
    over("conv_acc", [P, CT, AW], gates + 15 * T * 4 + (CT * YW * 4 + 31) // 32 * 32)
    assert CT * (YW + AW) + 8 <= 9 * T
    over("fac0", [P, 2, 2, NT, P], gla)
    over("gqk", [P, 2, 2, T], gla + 2 * 2 * T * 4)
    over("fac1", [P, 2, 2, NT, P], diff)
    over("gv", [P, NT, 512], diff_lo)
    over("attn", [P, NT, H, P], conv)
    over("cross", [P, 2, H, P], conv_lo)
    over("state0", [P, 2, 2, P], conv_lo + 2 * H * P * 4)
    over("conv_z", [P, CT, T], conv_lo)
    over("conv_s", [P, CT, T], conv)
    prefix = own("prefix", [P, 2, 2, NT, P + 1])
    over("prob", [P, 2, T], prefix)
    over("probT", [P, 2, NT, P], prefix + 2 * T * 4)
    gg = own("gg", [P, H, T])
    own("dqk", [P, 2, H, T])
    dv = own("dv", [P, NT, 512])
    over("ck_rows", [P, 512], dv)
    own("cv", [P, 512])
    own("ckT", [P, H, P])
    over("mod_w", [P, MODR, 2, 512], gg)
    over("acc", [P, 2, 2, 512], gg + MODR * 4096)
    assert (MODR + 2) * 4096 <= (H + 2 * H) * T * 4 + NT * 512 * 4 + 512 * 4
    sq = own("sq", [P, 2, T])
    over("stateT", [P, 2, P], sq)
    over("state_out", [DK, H, P], sq + 2 * P * 4)
    t = own("t", [P, 2, T])
    over("lrT", [2 * RANK, T], t)
    over("q_enter", [P, 2, 2, P], t)
    own("rstd", [P, T])
    own("rope", [P, 2, TS])
    own("swap", [P, P])
    own("ident", [P, P])
    own("ones", [P, P])
    own("masks", [P, LEVELS, P], U8)
    own("wa", [2 * RANK, 2, 256])
    own("rows", [P, 2, P])
    own("prm", [P, R_END])
    own("cw", [P, TAPS * CT])
    own("csil", [P, 16])
    own("mod_sum", [P, 48, 2])
    own("mod", [P, 48, 2])
    own("eff", [P, 2, KD, 2])
    own("lam", [P, 4, DK])
    own("lam2", [P, 8])
    own("lamc", [P, 2])
    own("subg", [P, 1])
    own("eps", [P, 1])
    own("one", [P, 1])
    own("mx", [P, 8])
    own("etot", [P, 4])
    assert top[0] <= nc.sbuf_usable_end, (top[0], nc.sbuf_usable_end)
    return m


def program(nc, x_prompt, x_sample, cache_diff_k, cache_diff_v, state_gla, c, c_ctx, w_mod, b_mod, norm1_g, norm2_g,
            w_in, gla_w_a2, gla_b_a, gla_norm_g, conv_w, conv_b, conv_ln_g, conv_ln_b, diff_lambda, diff_subln_g,
            w_branch, w_out, w_ffn_in, w_ffn_out, final_norm_g, k_rope, k_swap, k_ident, k_masks, k_lam,
            y_prompt, y_sample, new_k, new_v, new_s):
    with ExitStack() as ctx:
        m = memory(nc)
        ps = ctx.enter_context(nc.psum_tensor("ps", [P, 8, 512], F32))
        pair = [ps[:, 2 * i:2 * i + 2, 0:T] for i in range(4)]
        flat = [ps[:, 2 * i:2 * i + 2, :].rearrange("p a b -> p (a b)") for i in range(4)]

        def signal(name, per=1, credit=0):
            return Signal(nc, ctx, name, per, credit)

        raw_full = [signal(f"raw_full{i}", 16 * PIECES // RAW) for i in range(RAW)]
        hi_ready = signal("hi_ready", PIECES, RAW)
        lo_ready = signal("lo_ready", PIECES, RAW)
        piece_used = signal("piece_used", PIECES, SPL)
        mod_full = [signal(f"mod_full{i}", 16 * MOD_CHUNKS, 16 * MOD_CHUNKS) for i in range(MODR)]
        mod_mac = signal("mod_mac", 2 * KD * MOD_CHUNKS, 2 * (KD - MOD_PE) * MOD_CHUNKS)
        mod_part = signal("mod_part", 1)
        mod_red = signal("mod_red", MOD_CHUNKS, MOD_CHUNKS)
        mod_out = signal("mod_out", MOD_CHUNKS, MOD_CHUNKS)
        const_in = signal("const_in")
        first_in = signal("first_in")
        start_v = signal("start_v")
        masks_v = signal("masks_v")
        start_a = signal("start_a")
        start_p = signal("start_p")
        rows_in = signal("rows_in", 16 * 11)
        wa_in = signal("wa_in", 32)
        ctx_in = signal("ctx_in", 16 * 4)
        state_in = signal("state_in", 16 * 4)
        rows_t = signal("rows_t", 1, 1)
        keys_t = signal("keys_t")
        small_v = signal("small_v", 3)
        setup_v = signal("setup_v", 8, 1)
        setup_a = signal("setup_a")
        x_part = signal("x_part", 2 * KD)
        x_ready = signal("x_ready", 2 * KD)
        sq_ready = signal("sq_ready", 2 * KD)
        sq_used = signal("sq_used", 2 * KD, 2)
        rstd_a = signal("rstd_a", 4)
        t_ready = signal("t_ready", 4 * KD)
        h_hi_ready = signal("h_hi_ready", 4 * KD)
        h_lo_ready = signal("h_lo_ready", 4 * KD)
        pair_read = [signal("pair_read0", 15), signal("pair_read1", 14)]
        gg_sig = signal("gg_sig", 2)
        pads = signal("pads", 3)
        y_prompt_ready = signal("y_prompt_ready", 2)
        tap = signal("tap", TAPS * CT)
        mean_done = signal("mean_done")
        centred = signal("centred", CT)
        csq = signal("csq", CT)
        csq_used = signal("csq_used", CT)
        crstd = signal("crstd", 2)
        conv_normed = signal("conv_normed", 2 * CT)
        conv_sig = signal("conv_sig", CT)
        conv_out = signal("conv_out", CT)
        conv_hi_a = signal("conv_hi_a")
        conv_lo_v = signal("conv_lo_v")
        z_done = signal("z_done", 1, 1)
        zb = signal("zb", 4)
        za = signal("za", 3)
        decay = signal("decay", 2)
        scan = signal("scan", 12)
        etot_a = signal("etot_a", 2)
        built = signal("built", 4 * LEVELS + 4)
        expd = signal("expd", ROUNDS)
        factors = signal("factors", ROUNDS)
        level_done = signal("level_done", ROUNDS + 1)
        even_heads = signal("even_heads", ROUNDS + 1)
        copied = signal("copied", 3 * (LEVELS + 1) + 2)
        entered = signal("entered", 4)
        st_t = signal("st_t", 2)
        st_c = signal("st_c", 2)
        st_mm = signal("st_mm", 2)
        st_v = signal("st_v", 2)
        st_out = signal("st_out", 32)
        o_done = signal("o_done", H)
        osq = signal("osq", 2 * H)
        oss = signal("oss", 2 * H)
        orstd = signal("orstd", 4 * H)
        o_mul = signal("o_mul", 3 * H)
        o_copy = signal("o_copy", H)
        o_hi = signal("o_hi", 2)
        o_lo = signal("o_lo", 2)
        rot_done = signal("rot_done", 4)
        roped = signal("roped", 12)
        kT_done = signal("kT_done")
        k_rows = signal("k_rows")
        kv_out = signal("kv_out", 32, 1)
        sc_done = signal("sc_done", 12)
        mx_v = signal("mx_v", 24)
        ex_a = signal("ex_a", 24)
        w_v = signal("w_v", 48)
        tp_done = signal("tp_done", 12)
        wt_a = signal("wt_a", 12)
        pv_done = signal("pv_done", 12, 1)
        gsig = signal("gsig", 3)
        gated = signal("gated", N_BR)
        summed = signal("summed", 8)
        merged_a = signal("merged_a", 4)
        merged_v = signal("merged_v", 4)
        silu_a = signal("silu_a", PAIRS, 1)
        u_v = signal("u_v", PAIRS, 1)
        uhi_a = signal("uhi_a", PAIRS)
        ulo_v = signal("ulo_v", PAIRS, 1)
        fin_a = signal("fin_a")
        fin_v = signal("fin_v")
        fin_p = signal("fin_p")
        y_out = signal("y_out")

        def keys_of(q):
            return P if q == 0 else T

        block = ctx.enter_context(nc.Block())

        @block.sync
        def _(sp):
            sp.sem_inc(kv_out.sem, 1)
            for src, dst in ((k_ident, "ident"), (k_rope, "rope"), (k_swap, "swap"), (k_masks, "masks_in")):
                sp.dma_start(m[dst][:], src).then_inc(const_in.sem, 16)
            sp.dma_start(m["rows"][0:8, 0, :], c_ctx.rearrange("(k p) -> k p", p=P)).then_inc(first_in.sem, 16)
            sp.dma_start(m["rows"][8:16, 0, :], c.rearrange("b (k p) -> (b k) p", p=P)).then_inc(first_in.sem, 16)
            sp.dma_start(m["stage"][:, 0, :], x_prompt[0]).then_inc(first_in.sem, 16)
            sp.dma_start(m["stage"][:, 1:3, :], x_sample[0].rearrange("(t p) d -> p t d", p=P)).then_inc(first_in.sem, 16)

            def mod_piece(layer, col, j):
                sp.dma_start(m["mod_w"][:, j], w_mod[layer, 256 * j:256 * j + 256, col].rearrange("(k p) n -> p k n", p=P)
                             ).then_inc(mod_full[j].sem, 16)

            macs = 2 * (KD - MOD_PE)
            for n in range(MOD_CHUNKS):
                for j in range(MODR):
                    if n:
                        if 2 * j < MOD_PE:
                            sp.wait_ge(mod_part.sem, n)
                        if 2 * j + 2 > MOD_PE:
                            sp.wait_ge(mod_mac.sem, macs * (n - 1) + 2 * (2 * j + 2 - MOD_PE))
                    mod_piece(0, slice(512 * n, 512 * n + 512), j)

            with sp.Fori(0, DEPTH) as l:
                sp.get_value_cache().nocache = True
                def piece(s, src):
                    sp.wait_ge(*hi_ready.at(l, s - RAW + 1))
                    sp.wait_ge(*lo_ready.at(l, s - RAW + 1))
                    k, n = src.shape[0] // P, src.shape[1]
                    sp.dma_start(m["w_raw"][:, s % RAW, 0:k * n].rearrange("p (k n) -> p k n", k=k),
                                 src.rearrange("(k p) n -> p k n", p=P)).then_inc(raw_full[s % RAW].sem, 16)

                sp.wait_ge(start_p.sem, 1)
                sp.wait_ge(*rows_t.at(l, 0))
                row = 0
                for src in (b_mod[l].rearrange("(r p) -> r p", p=P), norm1_g[l].rearrange("(r p) -> r p", p=P),
                            norm2_g[l].rearrange("(r p) -> r p", p=P),
                            gla_b_a[l].rearrange("d (r p) -> (d r) p", p=P), gla_norm_g[l].rearrange("(r p) -> r p", p=P),
                            conv_b[l].rearrange("(r p) -> r p", p=P), conv_ln_g[l].rearrange("(r p) -> r p", p=P),
                            conv_ln_b[l].rearrange("(r p) -> r p", p=P), diff_subln_g[l].rearrange("(r p) -> r p", p=P),
                            final_norm_g.rearrange("(r p) -> r p", p=P)):
                    sp.dma_start(m["rows"][row:row + src.shape[0], 0, :], src).then_inc(rows_in.sem, 16)
                    row += src.shape[0]
                assert row == R_END
                sp.dma_start(m["rows"][0:TAPS * CT, 1, :], conv_w[l].rearrange("w (r p) -> (w r) p", p=P)
                             ).then_inc(rows_in.sem, 16)
                for s in range(N_IN):
                    col, width = IN_CHUNKS[s // 2]
                    half = s % 2
                    piece(s, w_in[l, half * 512:(half + 1) * 512, col:col + width])
                    if s == 2:
                        sp.wait_ge(start_v.sem, 4)
                        sp.wait_ge(*z_done.at(l, 0))
                        sp.dma_start(m["wa"][0:RANK, 0, :], gla_w_a2[l, 0]).then_inc(wa_in.sem, 16)
                        sp.dma_start(m["wa"][RANK:2 * RANK, 1, :], gla_w_a2[l, 1]).then_inc(wa_in.sem, 16)
                        sp.wait_ge(*mod_red.at(l, 0))
                        sp.dma_start(m["ck_rows"][:], cache_diff_k[0, l].rearrange("t h j d -> t (h j d)")
                                     ).then_inc(ctx_in.sem, 16)
                        sp.dma_start(m["cv"][:], cache_diff_v[0, l].rearrange("t h d -> t (h d)")).then_inc(ctx_in.sem, 16)
                        sp.wait_ge(*setup_v.at(l, 0))
                        sp.dma_start(m["lam"][:], diff_lambda[l].partition_broadcast(P)).then_inc(ctx_in.sem, 16)
                        sp.dma_start(m["lamc"][:], k_lam[l].partition_broadcast(P)).then_inc(ctx_in.sem, 16)
                    if s == 6:
                        sp.wait_ge(*x_ready.at(l, KD))
                        for d in range(2):
                            for hh in range(2):
                                sp.dma_start(m["state0"][DK * hh:DK * hh + DK, d, :, :],
                                             state_gla[0, l, d].rearrange("(t s) k v -> s k t v", s=2)[hh]
                                             ).then_inc(state_in.sem, 16)
                    if s == 39:
                        sp.wait_ge(*pair_read[0].at(l, 9))
                        sp.wait_ge(*pair_read[1].at(l, 8))
                        sp.dma_start(new_v[0, l].rearrange("t h d -> t (h d)"), m["dv"][:, 0, :]).then_inc(kv_out.sem, 16)
                    if s == 42:
                        sp.wait_ge(*k_rows.at(l, 1))
                        sp.dma_start(new_k[0, l].rearrange("t h j d -> t (h j d)"), m["k_rows"][:]
                                     ).then_inc(kv_out.sem, 16)
                    if s in (44, 46):
                        d = (s - 44) // 2
                        sp.wait_ge(*st_v.at(l, d + 1))
                        sp.dma_start(new_s[0, l, d].rearrange("h k v -> k h v"), m["state_out"][:]).then_inc(st_out.sem, 16)
                for n in range(N_BR):
                    mc, b = n // 3, (0, 2, 1)[n % 3]
                    piece(BR0 + n, w_branch[l, b * 512:(b + 1) * 512, 256 * mc:256 * mc + 256])
                sp.wait_ge(*pv_done.at(l, 12))
                sp.wait_ge(*o_lo.at(l, 2))
                sp.wait_ge(*kv_out.at(l, 32))
                for s in range(N_WO):
                    half = s % 2
                    piece(WO0 + s, w_out[l, half * 512:(half + 1) * 512, 256 * (s // 2):256 * (s // 2) + 256])
                following = (l + 1) % DEPTH
                with sp.Fori(0, PAIRS) as i:
                    sp.get_value_cache().nocache = True
                    for j in range(4):
                        half, part = j % 2, j // 2
                        s = FI0 + j
                        sp.wait_ge(hi_ready.sem, l * PIECES + i * 4 + (s + 1))
                        sp.wait_ge(lo_ready.sem, l * PIECES + i * 4 + (s + 1))
                        sp.dma_start(m["w_raw"][:, s % RAW, :].rearrange("p (k n) -> p k n", k=4),
                                     w_ffn_in[l, half * 512:(half + 1) * 512, bass.ds(i * 256 + part * HID, 256)]
                                     .rearrange("(k p) n -> p k n", p=P)).then_inc(raw_full[s % RAW].sem, 16)
                        sp.wait_ge(mod_mac.sem, l * mod_mac.per + i * 2 * KD + (mod_mac.credit - 2 * KD + 4 * (j + 1)))
                        mod_piece(following, bass.ds(i * 512, 512), j)
                for s in range(N_FO):
                    g, kk = s // 11, s % 11
                    piece(FO0 + s, w_ffn_out[l, kk * 256:(kk + 1) * 256, 512 * g:512 * g + 512])
                    if s < MODR:
                        sp.wait_ge(*mod_mac.at(l, 2 * KD * (PAIRS - 1) + 4 * (s + 1)))
                        mod_piece(following, slice(512 * PAIRS, 512 * PAIRS + 512), s)
            for tt in range(NT):
                sp.wait_ge(fin_v.sem, KD + tt + 1)
                dst = y_prompt[0] if tt == 0 else y_sample[0, (tt - 1) * P:tt * P]
                sp.dma_start(dst, m["stage"][:, tt, :]).then_inc(y_out.sem, 16)
            sp.wait_ge(*kv_out.at(DEPTH, 0))
            sp.wait_ge(st_out.sem, 32 * DEPTH)
            sp.wait_ge(y_out.sem, 16 * NT)

        @block.gpsimd
        def _(pool):
            pool.sem_inc(lo_ready.sem, RAW)
            with pool.Fori(0, DEPTH * PIECES // 4) as g:
                pool.get_value_cache().nocache = True
                for j in range(4):
                    pool.wait_ge(raw_full[j % RAW].sem, g * (16 * 4 // RAW) + 16 * (j // RAW + 1))
                    pool.wait_ge(hi_ready.sem, g * 4 + (j + 1 + RAW))
                    nc.gpsimd.tensor_tensor(m["w_lo"][:, j], m["w_raw"][:, j % RAW], m["w_hi"][:, j].bitcast(F32),
                                            ALU.subtract).then_inc(lo_ready.sem, 1)

        @block.tensor
        def _(pe):
            mm = nc.tensor.matmul
            ident, ones = m["ident"], m["ones"]
            pe.sem_inc(piece_used.sem, SPL)
            pe.sem_inc(sq_used.sem, 2)
            pe.sem_inc(rows_t.sem, 1)
            pe.sem_inc(z_done.sem, 1)
            pe.sem_inc(pv_done.sem, 1)
            pe.wait_ge(const_in.sem, 64)
            pe.wait_ge(first_in.sem, 64)
            nc.tensor.transpose(ps[:, 7, T:T + 16], m["rows"][0:16, 0, :], ident[0:16, 0:16]).then_inc(start_p.sem, 1)
            for k in range(KD):
                if k == 7:
                    pe.wait_ge(start_v.sem, 5)
                for tt in range(NT):
                    ins = nc.tensor.transpose(ps[:, k, tt * P:tt * P + P], m["stage"][:, tt, k * P:k * P + P], ident[:])
                ins.then_inc(start_p.sem, 1)

            cond = m["csil"][:].rearrange("p (j k) -> p k j", k=KD)

            def mod_sums(bank, acc, start):
                for t4 in range(4):
                    for j in range(2):
                        ins = mm(ps[:, bank, 2 * t4 + j:2 * t4 + j + 1], acc[:, j, P * t4:P * t4 + P], ones[:, 0:1],
                                 start=start, stop=True, skip_group_check=True)
                ins.then_inc(mod_red.sem, 1)

            pe.wait_ge(x_ready.sem, KD)
            for c in range(MOD_CHUNKS + 1):
                if c >= 2:
                    pe.wait_ge(mod_out.sem, c - 1)
                for k in range(MOD_PE if c < MOD_CHUNKS else 0):
                    if k % 2 == 0:
                        pe.wait_ge(mod_full[k // 2].sem, 16 * (c + 1))
                    for t4 in range(4):
                        ins = mm(ps[:, 6 + c % 2, 2 * t4:2 * t4 + 2], m["mod_w"][:, k // 2, k % 2, P * t4:P * t4 + P],
                                 cond[:, k, :], start=k == 0 and t4 == 0, stop=False, skip_group_check=True)
                if c < MOD_CHUNKS:
                    ins.then_inc(mod_part.sem, 1)
                if c:
                    pe.wait_ge(mod_mac.sem, 2 * (KD - MOD_PE) * c)
                    mod_sums(6 + (c - 1) % 2, m["acc"][:, (c - 1) % 2], False)

            with pe.Fori(0, DEPTH) as l:
                pe.get_value_cache().nocache = True
                def mix(s, lhs_j, outs, k, rhs, start, stop):
                    ins = None
                    hi, lo = m["w_hi"][:, s % SPL, :], m["w_lo"][:, s % SPL, :]
                    for out, at in zip(outs, lhs_j):
                        mm(out, hi[:, at:at + P], rhs[0][:, k, :], start=start, stop=False)
                        mm(out, hi[:, at:at + P], rhs[1][:, k, :], start=False, stop=False)
                        ins = mm(out, lo[:, at:at + P], rhs[0][:, k, :], start=False, stop=stop)
                    return ins

                def split(s):
                    pe.wait_ge(*hi_ready.at(l, s + 1))
                    pe.wait_ge(*lo_ready.at(l, s + 1))

                h = (m["h_hi"], m["h_lo"])

                def square_sum(i):
                    pe.wait_ge(*sq_ready.at(l, i + 1))
                    if i == KD:
                        pe.wait_ge(*gated.at(l, N_BR))
                    mm(ps[:, 4 * (i // KD), 0:T], ones[:], m["sq"][:, i % 2, :], start=i % KD == 0,
                       stop=i % KD == KD - 1).then_inc(sq_used.sem, 1)

                for k in range(KD):
                    square_sum(k)
                pe.wait_ge(*rows_in.at(l, 16 * 11))
                pe.wait_ge(*x_ready.at(l, KD))
                nc.tensor.transpose(ps[:, 5, 0:R_END], m["rows"][0:R_END, 0, :], ident[0:R_END, 0:R_END])
                nc.tensor.transpose(ps[:, 5, P:P + TAPS * CT], m["rows"][0:TAPS * CT, 1, :],
                                    ident[0:TAPS * CT, 0:TAPS * CT]).then_inc(rows_t.sem, 1)

                def chunk_piece(s):
                    c, half = s // 2, s % 2
                    col, width = IN_CHUNKS[c]
                    split(s)
                    if half == 0 and c >= 2:
                        pe.wait_ge(*pair_read[c % 2].at(l, c // 2))
                    out = pair[c % 2]
                    ins = None
                    if c == 6:
                        for j in range(4):
                            k = 4 * half + j
                            o = out[0:2 * RANK, 0, :]
                            w = [m[n][:, s % SPL, j * 32:j * 32 + 32] for n in ("w_hi", "w_lo")]
                            mm(o, w[0], h[0][:, k, :], start=k == 0, stop=False)
                            mm(o, w[0], h[1][:, k, :], start=False, stop=False)
                            ins = mm(o, w[1], h[0][:, k, :], start=False, stop=k == KD - 1)
                    elif col in (C_GV, C_GV + 256, C_DV, C_DV + 256):
                        for j in range(4):
                            k = 4 * half + j
                            w = [m[n][:, s % SPL, j * 256:j * 256 + 256] for n in ("w_hi", "w_lo")]
                            for tt in range(NT):
                                o = flat[c % 2][:, tt * 256:tt * 256 + 256]
                                x = [h[i][:, k, tt * P:tt * P + P] for i in range(2)]
                                mm(o, x[0], w[0], start=k == 0 and tt != 1, stop=False, skip_group_check=True)
                                mm(o, x[0], w[1], start=False, stop=False, skip_group_check=True)
                                ins = mm(o, x[1], w[0], start=False, stop=k == KD - 1, skip_group_check=True)
                    else:
                        for j in range(4):
                            k = 4 * half + j
                            if c == 0:
                                pe.wait_ge(*h_lo_ready.at(l, 2 * (k + 1)))
                            ins = mix(s, [j * 256, j * 256 + P], [out[:, 0, :], out[:, 1, :]], k, h, k == 0, k == KD - 1)
                    ins.then_inc(piece_used.sem, 1)

                def heads(bank):
                    return [ps[:, bank, P * hh:P * hh + P] for hh in range(H)]

                def part(name, side, hh, tt):
                    rows = slice(DK * (hh % 2), DK * (hh % 2) + DK)
                    x = m[name]
                    if name == "gqk":
                        return x[rows, side, hh // 2, tt * P:tt * P + P]
                    return x[rows, side, hh // 2, tt, :]

                def even_heads_done(ins, n):
                    ins.then_inc(even_heads.sem, 1)
                    pe.wait_ge(*even_heads.at(l, n))

                def level(i):
                    if i >= 0:
                        pe.wait_ge(*factors.at(l, i + 1))
                        pe.wait_ge(*copied.at(l, 3 * (i + 1)))
                    else:
                        pe.wait_ge(*zb.at(l, 4))
                        pe.wait_ge(*pair_read[1].at(l, 4))
                        pe.wait_ge(*pair_read[0].at(l, 5))
                    for odd in range(2):
                        for tt in range(NT):
                            for hh in (odd, odd + 2):
                                out = heads(4 + tt)[hh]
                                if i < 0:
                                    mm(out, part("gqk", 1, hh, tt), part("gqk", 0, hh, tt), start=True, stop=False)
                                    ins = mm(out, part("gqk", 1, hh, tt), part("gqk", 0, hh, tt), start=False, stop=True)
                                else:
                                    f = f"fac{i % 2}"
                                    ins = mm(out, part(f, 1, hh, tt), part(f, 0, hh, tt), start=True, stop=True)
                        if odd == 0:
                            even_heads_done(ins, i + 2)
                    ins.then_inc(level_done.sem, 1)

                def whole(d):
                    i = LEVELS + d
                    f, kt, qt = f"fac{i % 2}", 1 + d, 2 - d
                    pe.wait_ge(*factors.at(l, i + 1))
                    pe.wait_ge(*copied.at(l, 3 * (LEVELS + 1)))
                    for hh in (0, 2, 1, 3):
                        ins = mm(heads(4 + d)[hh], part(f, 1, hh, kt), part(f, 0, hh, qt), start=True, stop=True)
                        if hh == 2:
                            even_heads_done(ins, LEVELS + 2 + d)
                    ins.then_inc(level_done.sem, 1)
                    if d:
                        pe.wait_ge(*st_c.at(l, 1))
                    for ht in range(2):
                        ins = nc.tensor.transpose(ps[:, 6, (2 * d + ht) * P:(2 * d + ht) * P + P],
                                                  m[f][:, 1, ht, 0, :], ident[:])
                    ins.then_inc(st_t.sem, 1)

                def state(d):
                    pe.wait_ge(*st_c.at(l, d + 1))
                    pe.wait_ge(*pair_read[1].at(l, 5))
                    pe.wait_ge(*pair_read[0].at(l, 6))
                    pe.wait_ge(*k_rows.at(l, 1))
                    if d:
                        pe.wait_ge(*st_v.at(l, 1))
                    for hh in range(H):
                        lo = DK * (hh % 2)
                        ins = mm(ps[0:DK, 7, P * hh:P * hh + P], m["stateT"][:, hh // 2, lo:lo + DK],
                                 m["gv"][:, 0, P * hh:P * hh + P], start=True, stop=True)
                    ins.then_inc(st_mm.sem, 1)

                def gla_out(hh):
                    rows = slice(DK * (hh % 2), DK * (hh % 2) + DK)
                    cols = slice(P * hh, P * hh + P)
                    bank = 4 + hh % 2
                    if hh == 0:
                        pe.wait_ge(*copied.at(l, 3 * (LEVELS + 1) + 2))
                        pe.wait_ge(*entered.at(l, 4))
                        pe.wait_ge(*state_in.at(l, 64))
                    if hh >= 2:
                        pe.wait_ge(*o_mul.at(l, 2 * (hh - 1)))
                    v, att, cr, s0 = m["gv"], m["attn"], m["cross"], m["state0"]
                    mm(ps[:, bank, 0:P], v[:, 0, cols], att[:, 0, hh, :], start=True, stop=True)
                    o = ps[:, bank, P:2 * P]
                    mm(o, v[:, 1, cols], att[:, 1, hh, :], start=True, stop=False)
                    mm(o, v[:, 2, cols], cr[:, 1, hh, :], start=False, stop=False)
                    mm(o, s0[rows, 0, hh // 2, :], part("fac1", 0, hh, 1), start=False, stop=False)
                    mm(o, s0[rows, 1, hh // 2, :], m["q_enter"][rows, 1, hh // 2, :], start=False, stop=True)
                    o = ps[:, bank, 2 * P:3 * P]
                    mm(o, v[:, 2, cols], att[:, 2, hh, :], start=True, stop=False)
                    mm(o, v[:, 1, cols], cr[:, 0, hh, :], start=False, stop=False)
                    mm(o, s0[rows, 0, hh // 2, :], m["q_enter"][rows, 0, hh // 2, :], start=False, stop=False)
                    mm(o, s0[rows, 1, hh // 2, :], part("fac0", 0, hh, 2), start=False, stop=True).then_inc(o_done.sem, 1)

                def head_square_sum(n):
                    pe.wait_ge(*osq.at(l, n + 1))
                    if n == 0:
                        pe.wait_ge(*st_c.at(l, 2))
                    if n >= H:
                        pe.wait_ge(*wt_a.at(l, min(3 * (n - H) + 5, 12)))
                    mm(ps[:, 6, 0:T], ones[:], m["rstd"][:], start=True, stop=True).then_inc(oss.sem, 1)

                def rotate(r):
                    side, ht = r // 2, 2 * (r % 2)
                    pe.wait_ge(*pair_read[(11 + r) % 2].at(l, (11 + r) // 2 + 1))
                    if r == 0:
                        pe.wait_ge(*zb.at(l, 4))
                    else:
                        pe.wait_ge(*roped.at(l, 3 * r))
                    for j in range(2):
                        ins = mm(ps[:, 7, j * TS:j * TS + TS], m["swap"][:], m["dqk"][:, side, ht + j, TP:T],
                                 start=True, stop=True)
                    ins.then_inc(rot_done.sem, 1)

                def prompt_keys():
                    pe.wait_ge(*roped.at(l, 12))
                    for hh in range(H):
                        ins = nc.tensor.transpose(ps[:, 7, P * hh:P * hh + P], m["dqk"][:, 1, hh, 0:TP], ident[:])
                    ins.then_inc(kT_done.sem, 1)

                def scores(u):
                    hh, q = UNITS[u]
                    if u == 0:
                        pe.wait_ge(*o_mul.at(l, 2 * H))
                        pe.wait_ge(*small_v.at(l, 3))
                    else:
                        pe.wait_ge(*ex_a.at(l, 2 * u))
                    for t in range(2):
                        rows = slice(DK * t, DK * t + DK)
                        qT = m["dqk"][rows, 0, hh, P * q:P * q + P]
                        if q == 0:
                            ins = mm(ps[:, 4 + t, 0:P], qT, m["dqk"][rows, 1, hh, 0:P], start=True, stop=True)
                        else:
                            mm(ps[:, 4 + t, 0:TS], qT, m["dqk"][rows, 1, hh, TP:T], start=True, stop=True)
                            ins = mm(ps[:, 4 + t, TS:T], qT, m["ckT"][rows, hh, :], start=True, stop=True)
                    ins.then_inc(sc_done.sem, 1)

                def weights_T(u):
                    hh, q = UNITS[u]
                    pe.wait_ge(*w_v.at(l, 4 * (u + 1)))
                    if u == 0:
                        pe.wait_ge(*orstd.at(l, 2 * H))
                    else:
                        pe.wait_ge(*wt_a.at(l, u))
                    if u in (5, 8, 11):
                        pe.wait_ge(*orstd.at(l, 2 * (H + u // 3) - 1))
                    for kt in range(keys_of(q) // P):
                        ins = nc.tensor.transpose(ps[:, 6, P * kt:P * kt + P], m["prob"][:, 0, P * kt:P * kt + P], ident[:])
                    ins.then_inc(tp_done.sem, 1)

                def values(u):
                    hh, q = UNITS[u]
                    cols = slice(P * hh, P * hh + P)
                    pe.wait_ge(*wt_a.at(l, u + 1))
                    if u == 0:
                        pe.wait_ge(*crstd.at(l, 1))
                        pe.wait_ge(*pair_read[1].at(l, 8))
                        pe.wait_ge(*pair_read[0].at(l, 9))
                    elif q == 0:
                        pe.wait_ge(*o_copy.at(l, hh))
                    src = [m["dv"][:, 0, cols]] if q == 0 else [m["dv"][:, 1, cols], m["dv"][:, 2, cols], m["cv"][:, cols]]
                    for kt, v in enumerate(src):
                        ins = mm(ps[:, 7, P * q:P * q + P], v, m["probT"][:, u % 2, kt, :], start=kt == 0,
                                 stop=kt == len(src) - 1)
                    ins.then_inc(pv_done.sem, 1)

                def conv_mean():
                    pe.wait_ge(*tap.at(l, TAPS * CT))
                    pe.wait_ge(*st_v.at(l, 2))
                    for ct in range(CT):
                        ins = mm(ps[:, 7, 0:AW], ones[:], m["conv_acc"][:, ct, :], start=ct == 0, stop=ct == CT - 1)
                    ins.then_inc(mean_done.sem, 1)

                def conv_var():
                    pe.wait_ge(*centred.at(l, CT))
                    for ct in range(CT):
                        pe.wait_ge(*csq.at(l, ct + 1))
                        mm(ps[:, 7, 0:AW], ones[:], m["t"][:].rearrange("p a b -> p (a b)")[:, 0:AW], start=ct == 0,
                           stop=ct == CT - 1).then_inc(csq_used.sem, 1)

                for s in range(N_IN):
                    chunk_piece(s)
                    if s == 6:
                        pe.wait_ge(*ctx_in.at(l, 64))
                        for hh in range(H):
                            ins = nc.tensor.transpose(ps[:, 6, P * hh:P * hh + P], m["ck_rows"][:, P * hh:P * hh + P],
                                                      ident[:])
                        ins.then_inc(keys_t.sem, 1)
                    if s == 17:
                        pe.wait_ge(*pair_read[0].at(l, 4))
                        pe.wait_ge(*wa_in.at(l, 32))
                        pe.wait_ge(*small_v.at(l, 3))
                        for i in range(4):
                            ins = mm(ps[:, 4 + i, 0:T], m["wa"][:, i // 2, P * (i % 2):P * (i % 2) + P], m["lrT"][:],
                                     start=True, stop=True)
                        ins.then_inc(z_done.sem, 1)
                    if s == 19:
                        level(-1)
                    if s in range(21, 21 + 2 * LEVELS, 2):
                        level((s - 21) // 2)
                    if s in (35, 37):
                        whole((s - 35) // 2)
                    if s in (28, 30, 32, 34):
                        rotate((s - 28) // 2)
                    if s == 35:
                        prompt_keys()
                    if s in (36, 38):
                        state((s - 36) // 2)
                    if 39 <= s < 43:
                        gla_out(s - 39)
                    if 40 <= s < 44:
                        head_square_sum(s - 40)
                    if s == 43:
                        conv_mean()
                    if s == 45:
                        conv_var()
                    if s in (50, 53, 56):
                        head_square_sum(H + (s - 50) // 3)
                    if 46 <= s:
                        values(s - 46)
                    if 45 <= s < 57:
                        weights_T(s - 45)
                    if 44 <= s < 56:
                        scores(s - 44)

                branch_in = ((m["gla_hi"], m["gla_lo"]), (m["conv_hi"], m["conv_lo"]), (m["diff_hi"], m["diff_lo"]))
                for n in range(N_BR):
                    mc, b = n // 3, (0, 2, 1)[n % 3]
                    s = BR0 + n
                    split(s)
                    if n == 0:
                        pe.wait_ge(*pair_read[0].at(l, 15))
                        pe.wait_ge(*o_lo.at(l, 1))
                    if n == 1:
                        head_square_sum(2 * H - 1)
                        pe.wait_ge(*pair_read[1].at(l, 14))
                        pe.wait_ge(*o_lo.at(l, 2))
                    if n == 2:
                        pe.wait_ge(*conv_lo_v.at(l, 1))
                    if n >= 4:
                        pe.wait_ge(*gated.at(l, n - 3))
                    for j in range(4):
                        ins = mix(s, [j * 256, j * 256 + P], [pair[n % 4][:, 0, :], pair[n % 4][:, 1, :]], j, branch_in[b],
                                  j == 0, j == 3)
                    ins.then_inc(piece_used.sem, 1)
                for r in range(N_WO):
                    cc, half, s = r // 2, r % 2, WO0 + r
                    split(s)
                    pe.wait_ge(*merged_v.at(l, 2 + 2 * half))
                    if half == 0:
                        if cc < 2:
                            pe.wait_ge(*gated.at(l, 9 + cc))
                        else:
                            pe.wait_ge(*x_ready.at(l, KD + 2 * (cc - 1)))
                    for j in range(4):
                        k = 4 * half + j
                        ins = mix(s, [j * 256, j * 256 + P], [pair[cc % 2][:, 0, :], pair[cc % 2][:, 1, :]], k, h, k == 0,
                                  k == KD - 1)
                    ins.then_inc(piece_used.sem, 1)
                    if r == 3:
                        square_sum(KD)
                        square_sum(KD + 1)
                    if r == 5:
                        square_sum(KD + 2)
                        square_sum(KD + 3)
                for i in range(4, 8):
                    square_sum(KD + i)
                with pe.Fori(0, PAIRS) as i:
                    pe.get_value_cache().nocache = True
                    for half_chunk in range(4):
                        half, part_b = half_chunk % 2, half_chunk // 2
                        s = FI0 + half_chunk
                        pe.wait_ge(hi_ready.sem, l * PIECES + i * 4 + (s + 1 + RAW))
                        pe.wait_ge(lo_ready.sem, l * PIECES + i * 4 + (s + 1 + RAW))
                        if half_chunk == 0:
                            pe.wait_ge(silu_a.sem, l * PAIRS + (i + 1))
                        if half_chunk == 2:
                            pe.wait_ge(u_v.sem, l * PAIRS + (i + 1))
                        for j in range(4):
                            k = 4 * half + j
                            if part_b == 0:
                                pe.wait_ge(*h_lo_ready.at(l, 2 * KD + 2 * (k + 1)))
                            ins = mix(s, [j * 256, j * 256 + P], [pair[part_b][:, 0, :], pair[part_b][:, 1, :]], k, h,
                                      k == 0, k == KD - 1)
                        ins.then_inc(piece_used.sem, 1)
                        if half_chunk == 3:
                            pe.wait_ge(mod_mac.sem, l * mod_mac.per + i * 2 * KD + (mod_mac.credit + 2 * KD))
                            pe.wait_ge(mod_out.sem, l * MOD_CHUNKS + i + mod_out.credit)
                            mod_sums(7, m["acc"][:, 0], True)
                act = (m["act_hi"], m["act_lo"])
                pe.wait_ge(*silu_a.at(l, PAIRS))
                pe.wait_ge(*u_v.at(l, PAIRS))
                for r in range(N_FO):
                    g, kk, s = r // 11, r % 11, FO0 + r
                    split(s)
                    if g == 0:
                        pe.wait_ge(*ulo_v.at(l, kk + 1))
                    if r == 11:
                        pe.wait_ge(*mod_out.at(l, MOD_CHUNKS))
                    for j in range(2):
                        k = 2 * kk + j
                        ins = mix(s, [j * 512 + P * i for i in range(4)], [ps[:, 4 * g + i, 0:T] for i in range(4)], k,
                                  act, k == 0, k == KH - 1)
                    ins.then_inc(piece_used.sem, 1)
                    if r == 5:
                        pe.wait_ge(*mod_mac.at(l, mod_mac.per))
                        pe.wait_ge(*mod_out.at(l, PAIRS))
                        mod_sums(7, m["acc"][:, 0], True)

            for k in range(KD):
                pe.wait_ge(*sq_ready.at(DEPTH, k + 1))
                mm(ps[:, 0, 0:T], ones[:], m["sq"][:, k % 2, :], start=k == 0, stop=k == KD - 1).then_inc(sq_used.sem, 1)
            pe.wait_ge(fin_v.sem, KD)
            for tt in range(NT):
                for k in range(KD):
                    ins = nc.tensor.transpose(ps[:, 2 * (tt % 2) + k // 4, P * (k % 4):P * (k % 4) + P]
                                              if tt < 2 else ps[:, 6 + k // 4, P * (k % 4):P * (k % 4) + P],
                                              m["x"][:, k, tt * P:tt * P + P], ident[:])
                ins.then_inc(fin_p.sem, 1)

        @block.scalar
        def _(act):
            fn = nc.scalar.activation
            act.sem_inc(hi_ready.sem, RAW)
            act.sem_inc(silu_a.sem, 1)
            act.wait_ge(start_p.sem, 1)
            fn(m["csil"][:], ps[:, 7, T:T + 16], ACT.Sigmoid).then_inc(start_a.sem, 1)

            for c in range(MOD_CHUNKS):
                act.wait_ge(mod_red.sem, c + 1)
                fn(m["mod_sum"][:, 4 * c:4 * c + 4, :], ps[:, 6 + c % 2, 0:8].rearrange("p (a b) -> p a b", b=2), ACT.Copy
                   ).then_inc(mod_out.sem, 1)
            act.preload_act_table_set(LN_EXP)
            with act.Fori(0, DEPTH) as l:
                act.get_value_cache().nocache = True
                def high(s):
                    act.wait_ge(*raw_full[s % RAW].at(l, 16 * (s // RAW + 1)))
                    act.wait_ge(*piece_used.at(l, s - SPL + 1))
                    fn(m["w_hi"][:, s % SPL, :], m["w_raw"][:, s % RAW, :], ACT.Copy).then_inc(hi_ready.sem, 1)

                def square(i):
                    act.wait_ge(*x_ready.at(l, i + 1))
                    act.wait_ge(*sq_used.at(l, i - 1))
                    fn(m["sq"][:, i % 2, :], m["x"][:, i % KD, :], ACT.Square).then_inc(sq_ready.sem, 1)

                def inverse_rms(which):
                    act.wait_ge(*sq_used.at(l, KD * (which + 1)))
                    fn(m["rstd"][:], ps[:, 4 * which, 0:T], ACT.Ln, bias=m["eps"][:], scale=1.0 / D).then_inc(rstd_a.sem, 1)
                    act.wait_ge(*rstd_a.at(l, 2 * which + 1))
                    fn(m["rstd"][:], m["rstd"][:], ACT.Exp, scale=-0.5).then_inc(rstd_a.sem, 1)

                def h_high(which):
                    for k in range(KD):
                        act.wait_ge(*t_ready.at(l, 2 * (KD * which + k + 1)))
                        for j, cols in enumerate((slice(0, TP), slice(TP, T))):
                            fn(m["h_hi"][:, k, cols], m["t"][:, k % 2, cols], ACT.Identity,
                               bias=m["mod"][:, 24 * which + k, j:j + 1]).then_inc(h_hi_ready.sem, 1)

                def evacuate(c):
                    col, _ = IN_CHUNKS[c]
                    src, src2 = pair[c % 2], flat[c % 2]
                    if c in (0, 2, 6):
                        return
                    act.wait_ge(*piece_used.at(l, 2 * c + 2))
                    done = pair_read[c % 2].sem
                    if c in (1, 3):
                        if c == 3:
                            act.wait_ge(*pair_read[0].at(l, 1))
                        fn(m["sq"][:], src, ACT.Sigmoid).then_inc(done, 1)
                    elif c in (4, 5):
                        fn(m["gg"][:, 2 * (c - 4):2 * (c - 4) + 2, :], src, ACT.Sigmoid).then_inc(gg_sig.sem, 1)
                    elif c == 7:
                        fn(m["gqk"][:, 0, :, :], src, ACT.Copy, scale=DK ** -0.5).then_inc(done, 1)
                    elif c == 8:
                        fn(m["gqk"][:, 1, :, :], src, ACT.Copy).then_inc(done, 1)
                    elif c in (9, 10, 15, 16):
                        dst, half = (m["gv"], c - 9) if c < 11 else (m["dv"], c - 15)
                        if c == 15:
                            act.wait_ge(*keys_t.at(l, 1))
                        fn(dst[:, :, 256 * half:256 * half + 256], src2[:, 0:NT * 256].rearrange("p (t n) -> p t n", t=NT),
                           ACT.Copy).then_inc(done, 1)
                    elif c < 15:
                        side, ht = (c - 11) // 2, 2 * ((c - 11) % 2)
                        fn(m["dqk"][:, side, ht:ht + 2, :], src, ACT.Copy).then_inc(done, 1)
                    else:
                        i = 2 * (c - 17)
                        if i + 1 >= 15:
                            act.wait_ge(*conv_normed.at(l, 2 * CT))
                        fn(m["gates"][:, i:i + 2, :], src, ACT.Copy).then_inc(done, 1)

                def exp_level(i):
                    act.wait_ge(*built.at(l, 4 * (i + 1) if i < LEVELS else 4 * LEVELS + 2 * (i + 1 - LEVELS)))
                    f = m[f"fac{i % 2}"]
                    fn(f[:], f[:], ACT.Exp, scale=1.0 / 16).then_inc(expd.sem, 1)

                def head_squares(n):
                    if n < H:
                        act.wait_ge(*o_done.at(l, n + 1))
                        if n:
                            act.wait_ge(*o_mul.at(l, 2 * n))
                        fn(m["rstd"][:], ps[:, 4 + n % 2, 0:T], ACT.Square).then_inc(osq.sem, 1)
                    else:
                        act.wait_ge(*pv_done.at(l, 3 * (n - H + 1)))
                        act.wait_ge(*o_lo.at(l, 1))
                        fn(m["gg"][:, n - H, :], ps[:, 7, 0:T], ACT.Copy).then_inc(o_copy.sem, 1)
                        act.wait_ge(*o_copy.at(l, n - H + 1))
                        act.wait_ge(*o_mul.at(l, 2 * H + n - H))
                        fn(m["rstd"][:], m["gg"][:, n - H, :], ACT.Square).then_inc(osq.sem, 1)

                def head_rstd(n):
                    act.wait_ge(*oss.at(l, n + 1))
                    fn(m["rstd"][:], ps[:, 6, 0:T], ACT.Ln, bias=m["eps"][:], scale=1.0 / DV).then_inc(orstd.sem, 1)
                    act.wait_ge(*orstd.at(l, 2 * n + 1))
                    fn(m["rstd"][:], m["rstd"][:], ACT.Exp, scale=-0.5).then_inc(orstd.sem, 1)

                def exp_scores(u):
                    _, q = UNITS[u]
                    act.wait_ge(*mx_v.at(l, 2 * (u + 1)))
                    if u == 0:
                        act.wait_ge(*copied.at(l, 3 * (LEVELS + 1) + 2))
                        act.wait_ge(*etot_a.at(l, 2))
                    else:
                        act.wait_ge(*tp_done.at(l, u))
                    for t in range(2):
                        fn(m["prob"][:, t, 0:keys_of(q)], ps[:, 4 + t, 0:keys_of(q)], ACT.Exp, bias=m["mx"][:, 2 + t:3 + t],
                           scale=DK ** -0.5, accum_out=m["mx"][:, 4 + t:5 + t]).then_inc(ex_a.sem, 1)

                def weights_back(u):
                    _, q = UNITS[u]
                    act.wait_ge(*tp_done.at(l, u + 1))
                    if u >= 2:
                        act.wait_ge(*pv_done.at(l, u - 1))
                    n = keys_of(q) // P
                    fn(m["probT"][:, u % 2, 0:n, :], ps[:, 6, 0:n * P].rearrange("p (t n) -> p t n", t=n),
                       ACT.Copy).then_inc(wt_a.sem, 1)

                def high_of(name, src, ready, done):
                    act.wait_ge(*ready)
                    fn(m[name], src, ACT.Copy).then_inc(done.sem, 1)

                flat_t = m["t"][:].rearrange("p a b -> p (a b)")
                for s in range(SPL):
                    high(s)
                for k in range(KD):
                    square(k)
                inverse_rms(0)
                h_high(0)
                for s in range(SPL, BR0 + 5):
                    high(s)
                    if (s - 5) % 2 == 0 and 0 <= (s - 5) // 2 < len(IN_CHUNKS):
                        evacuate((s - 5) // 2)
                    if s == 18:
                        act.preload_act_table_set(LN_EXP)
                        act.wait_ge(*setup_v.at(l, 5))
                        fn(m["lam2"][:, 2:4], m["lam2"][:, 0:2], ACT.Exp).then_inc(setup_a.sem, 1)
                    if s == 21:
                        f0 = m["fac0"][:].rearrange("p a b c d -> p (a b c d)")
                        f1 = m["fac1"][:].rearrange("p a b c d -> p (a b c d)")
                        act.wait_ge(*zb.at(l, 4))
                        fn(f0, f1, ACT.Abs).then_inc(za.sem, 1)
                        act.wait_ge(*za.at(l, 1))
                        fn(f0, f0, ACT.Exp, scale=-1.0).then_inc(za.sem, 1)
                        act.wait_ge(*za.at(l, 2))
                        fn(f0, f0, ACT.Ln, bias=m["one"][:]).then_inc(za.sem, 1)
                    if s == 23:
                        act.wait_ge(*scan.at(l, 12))
                        for d in range(2):
                            fn(m["etot"][:, 2 * d:2 * d + 2], m["prefix"][:, d, :, 1 + d, P], ACT.Exp, scale=1.0 / 16
                               ).then_inc(etot_a.sem, 1)
                        exp_level(0)
                    if s == 24:
                        exp_level(1)
                    if s in range(26, 22 + 2 * ROUNDS, 2):
                        exp_level((s - 22) // 2)
                    if s == 39:
                        act.wait_ge(*kT_done.at(l, 1))
                        act.wait_ge(*kv_out.at(l, 0))
                        fn(m["k_rows"][:], ps[:, 7, :], ACT.Copy).then_inc(k_rows.sem, 1)
                    if 44 <= s < 48:
                        head_rstd(s - 44)
                    if 43 <= s < 47:
                        head_squares(s - 43)
                    if s == 48:
                        high_of_gla = m["gla_hi"][:]
                        act.wait_ge(*o_mul.at(l, 2 * H))
                        fn(high_of_gla, m["gg"][:], ACT.Copy).then_inc(o_hi.sem, 1)
                        for ct in range(CT):
                            act.wait_ge(*centred.at(l, ct + 1))
                            if ct:
                                act.wait_ge(*csq_used.at(l, ct))
                            fn(flat_t[:, 0:AW], m["conv_acc"][:, ct, :], ACT.Square).then_inc(csq.sem, 1)
                    if s == 49:
                        act.wait_ge(*csq_used.at(l, CT))
                        fn(flat_t[:, 0:AW], ps[:, 7, 0:AW], ACT.Ln, bias=m["eps"][:], scale=1.0 / CONV).then_inc(crstd.sem, 1)
                        act.wait_ge(*crstd.at(l, 1))
                        fn(flat_t[:, 0:AW], flat_t[:, 0:AW], ACT.Exp, scale=-0.5).then_inc(crstd.sem, 1)
                    if s in (54, 57, 60, 62):
                        head_rstd(H + (54, 57, 60, 62).index(s))
                    if 49 <= s < 61:
                        weights_back(s - 49)
                    if 48 <= s < 60:
                        exp_scores(s - 48)
                    if s in (52, 55, 58, 61):
                        head_squares(H + (s - 52) // 3)
                act.wait_ge(*o_mul.at(l, 3 * H))
                fn(m["diff_hi"][:], m["gg"][:], ACT.Copy).then_inc(o_hi.sem, 1)
                for ct in range(CT):
                    act.wait_ge(*conv_normed.at(l, 2 * (ct + 1)))
                    fn(m["conv_s"][:, ct, :], m["conv_z"][:, ct, :], ACT.Sigmoid, bias=m["prm"][:, R_LB + ct:R_LB + ct + 1]
                       ).then_inc(conv_sig.sem, 1)
                act.wait_ge(*pair_read[0].at(l, 15))
                act.wait_ge(*pair_read[1].at(l, 14))
                for n, b in enumerate((0, 2, 1)):
                    g = m["gates"][:, KD * b:KD * b + KD, :]
                    fn(g, g, ACT.Sigmoid).then_inc(gsig.sem, 1)
                    if n == 2:
                        act.preload_act_table_set(LN_EXP)
                    if n == 0:
                        act.wait_ge(*conv_out.at(l, CT))
                        fn(m["conv_hi"][:], m["conv_z"][:], ACT.Copy).then_inc(conv_hi_a.sem, 1)
                for s in range(BR0 + 5, FI0 + 4):
                    high(s)
                    if s in (65, 68, 71, 74):
                        mc = (s - 65) // 3
                        act.wait_ge(*summed.at(l, 2 * (mc + 1)))
                        fn(m["h_hi"][:, 2 * mc:2 * mc + 2, :], m["gates"][:, 2 * mc:2 * mc + 2, :], ACT.Copy
                           ).then_inc(merged_a.sem, 1)
                    if s in (76, 78, 80, 81):
                        i = KD + 2 * ((76, 78, 80, 81).index(s))
                        square(i)
                        square(i + 1)
                inverse_rms(1)
                h_high(1)
                act.preload_act_table_set("silu_and_others")
                with act.Fori(0, PAIRS) as i:
                    act.get_value_cache().nocache = True
                    for j in range(4):
                        s = FI0 + SPL + j
                        act.wait_ge(raw_full[s % RAW].sem, l * raw_full[0].per + i * (16 * 4 // RAW) + 16 * (s // RAW + 1))
                        act.wait_ge(piece_used.sem, l * PIECES + i * 4 + (s + 1))
                        fn(m["w_hi"][:, s % SPL, :], m["w_raw"][:, s % RAW, :], ACT.Copy).then_inc(hi_ready.sem, 1)
                        if j == 1:
                            act.wait_ge(piece_used.sem, l * PIECES + i * 4 + (FI0 + 2 + SPL))
                            act.wait_ge(ulo_v.sem, l * PAIRS + (i + 1))
                            fn(m["sq"][:], pair[0], ACT.Silu).then_inc(silu_a.sem, 1)
                        if j == 3:
                            act.wait_ge(u_v.sem, l * PAIRS + (i + 2))
                            fn(m["act_hi"][:, bass.ds(i * 2, 2), :], m["sq"][:], ACT.Copy).then_inc(uhi_a.sem, 1)
                act.preload_act_table_set(LN_EXP)
                for s in range(FO0 + SPL, PIECES):
                    high(s)

            for k in range(KD):
                act.wait_ge(*x_ready.at(DEPTH, k + 1))
                act.wait_ge(*sq_used.at(DEPTH, k - 1))
                fn(m["sq"][:, k % 2, :], m["x"][:, k, :], ACT.Square).then_inc(sq_ready.sem, 1)
            act.wait_ge(*sq_used.at(DEPTH, KD))
            fn(m["rstd"][:], ps[:, 0, 0:T], ACT.Ln, bias=m["eps"][:], scale=1.0 / D).then_inc(fin_a.sem, 1)
            act.wait_ge(fin_a.sem, 1)
            fn(m["rstd"][:], m["rstd"][:], ACT.Exp, scale=-0.5).then_inc(fin_a.sem, 1)

        @block.vector
        def _(dve):
            v = nc.vector
            for s in (setup_v, u_v, ulo_v):
                dve.sem_inc(s.sem, 1)
            v.memset(m["eps"][:], EPS).then_inc(start_v.sem, 1)
            v.memset(m["one"][:], 1.0).then_inc(start_v.sem, 1)
            v.memset(m["ones"][:], 1.0).then_inc(start_v.sem, 1)
            v.memset(m["wa"][:], 0.0).then_inc(start_v.sem, 1)
            dve.wait_ge(const_in.sem, 64)
            v.tensor_copy(m["masks"][:], m["masks_in"][:]).then_inc(masks_v.sem, 1)
            dve.wait_ge(start_a.sem, 1)
            v.tensor_tensor(m["csil"][:], m["csil"][:], ps[:, 7, T:T + 16], ALU.mult).then_inc(start_v.sem, 1)
            for k in range(KD):
                dve.wait_ge(start_p.sem, k + 2)
                v.tensor_copy(m["x"][:, k, :], ps[:, k, 0:T]).then_inc(x_ready.sem, 1)

            def mod_mac_op(n, k, j, acc, before):
                w, cond = m["mod_w"][:, k // 2, k % 2, :], m["csil"][:, KD * j + k:KD * j + k + 1]
                if n == 0:
                    v.tensor_scalar(acc[:, j, :], w, cond, None, ALU.mult).then_inc(mod_mac.sem, 1)
                else:
                    dve.wait_ge(mod_mac.sem, before + 2 * n + j - 1)
                    v.scalar_tensor_tensor(acc[:, j, :], w, cond, acc[:, j, :], ALU.mult, ALU.add).then_inc(mod_mac.sem, 1)

            dve.wait_ge(start_v.sem, 5)
            for c in range(MOD_CHUNKS):
                if c >= 2:
                    dve.wait_ge(mod_red.sem, c - 1)
                for k in range(MOD_PE, KD):
                    if k == MOD_PE or k % 2 == 0:
                        dve.wait_ge(mod_full[k // 2].sem, 16 * (c + 1))
                    for j in range(2):
                        mod_mac_op(k - MOD_PE, k, j, m["acc"][:, c % 2], 2 * (KD - MOD_PE) * c)

            with dve.Fori(0, DEPTH) as l:
                dve.get_value_cache().nocache = True
                def done(ins, sig, n=None):
                    ins.then_inc(sig.sem, 1)
                    dve.wait_ge(*sig.at(l, n or sig.next()))

                def column(r, n=1):
                    return m["prm"][:, r:r + n]

                def spread(ap, n):
                    return ap.unsqueeze(2).broadcast_to([ap.shape[0], ap.shape[1], n])

                SEGS = ((0, slice(0, TP)), (1, slice(TP, T)))

                def norm_t(which, k):
                    if k >= 2:
                        dve.wait_ge(*h_lo_ready.at(l, 2 * (KD * which + k - 1)))
                    for j, cols in SEGS:
                        done(v.scalar_tensor_tensor(m["t"][:, k % 2, cols], m["x"][:, k, cols], m["eff"][:, which, k, j:j + 1],
                                                    m["rstd"][:, cols], ALU.mult, ALU.mult), t_ready)

                def norm_low(which, k):
                    dve.wait_ge(*h_hi_ready.at(l, 2 * (KD * which + k + 1)))
                    for j, cols in SEGS:
                        v.scalar_tensor_tensor(m["h_lo"][:, k, cols], m["t"][:, k % 2, cols],
                                               m["mod"][:, 24 * which + k, j:j + 1],
                                               m["h_hi"][:, k, cols].bitcast(F32), ALU.add, ALU.subtract
                                               ).then_inc(h_lo_ready.sem, 1)

                def modulated_norm(which):
                    dve.wait_ge(*rstd_a.at(l, 2 * which + 2))
                    norm_t(which, 0)
                    for k in range(1, KD):
                        norm_t(which, k)
                        norm_low(which, k - 1)
                    norm_low(which, KD - 1)

                def add_to_x(tile, src, gate):
                    done(v.scalar_tensor_tensor(m["x"][:, tile, 0:TP], src[:, 0:TP], m["mod"][:, gate + tile, 0:1],
                                                m["x"][:, tile, 0:TP], ALU.mult, ALU.add), x_part)
                    done(v.scalar_tensor_tensor(m["x"][:, tile, TP:T], src[:, TP:T], m["mod"][:, gate + tile, 1:2],
                                                m["x"][:, tile, TP:T], ALU.mult, ALU.add), x_ready,
                         (KD if gate == 16 else 2 * KD) + tile + 1)

                taps_done = [0]

                def taps(n):
                    for i in range(taps_done[0], min(taps_done[0] + n, TAPS * CT)):
                        w, ct = i // CT, i % CT
                        src, acc, wt = m["conv_in"][:, ct, w:w + AW], m["conv_acc"][:, ct, :], m["cw"][:, i:i + 1]
                        if w:
                            dve.wait_ge(*tap.at(l, i - CT + 1))
                            v.scalar_tensor_tensor(acc, src, wt, acc, ALU.mult, ALU.add).then_inc(tap.sem, 1)
                        else:
                            v.tensor_scalar(acc, src, wt, column(R_CB + ct), ALU.mult, ALU.add).then_inc(tap.sem, 1)
                    taps_done[0] = min(taps_done[0] + n, TAPS * CT)

                dve.wait_ge(masks_v.sem, 1)
                dve.wait_ge(*mod_out.at(l, 0))
                dve.wait_ge(*rows_t.at(l, 1))
                done(v.tensor_copy(m["prm"][:], ps[:, 5, 0:R_END]), small_v)
                done(v.tensor_copy(m["cw"][:], ps[:, 5, P:P + TAPS * CT]), small_v)
                done(v.tensor_tensor(m["mod"][:], m["mod_sum"][:], spread(column(R_BMOD, 48), 2), ALU.add), setup_v)
                done(v.scalar_tensor_tensor(m["eff"][:, 0, :, :], m["mod"][:, 8:16, :], 1.0, spread(column(R_N1, 8), 2),
                                            ALU.add, ALU.mult), setup_v)
                done(v.scalar_tensor_tensor(m["eff"][:, 1, :, :], m["mod"][:, 32:40, :], 1.0, spread(column(R_N2, 8), 2),
                                            ALU.add, ALU.mult), setup_v)
                modulated_norm(0)
                for a, b in ((0, PAD), (PAD + TP, Y_S), (Y_S + TS, YW)):
                    done(v.memset(m["conv_in"][:, :, a:b], 0.0), pads)

                for i in range(2):
                    dve.wait_ge(*piece_used.at(l, 4 * i + 2))
                    dve.wait_ge(*pair_read[1].at(l, i + 1))
                    tiles = slice(2 * i, 2 * i + 2)
                    done(v.tensor_tensor(m["conv_in"][:, tiles, Y_P:Y_P + TP], pair[0][:, :, 0:TP], m["sq"][:, :, 0:TP],
                                         ALU.mult), y_prompt_ready)
                    done(v.tensor_tensor(m["conv_in"][:, tiles, Y_S:Y_S + TS], pair[0][:, :, TP:T], m["sq"][:, :, TP:T],
                                         ALU.mult), pair_read[0], i + 1)
                dve.wait_ge(*keys_t.at(l, 1))
                done(v.tensor_copy(m["ckT"][:], ps[:, 6, :].rearrange("p (a b) -> p a b", a=H)), small_v)
                taps(8)
                for i in range(2):
                    dve.wait_ge(*gg_sig.at(l, i + 1))
                    g = m["gg"][:, 2 * i:2 * i + 2, :]
                    done(v.tensor_tensor(g, g, pair[i], ALU.mult), pair_read[i], 3)
                    taps(12)
                dve.wait_ge(*piece_used.at(l, 14))
                done(v.tensor_copy(m["lrT"][:], pair[0][0:2 * RANK, 0, :]), pair_read[0], 4)
                taps(12)
                lam = m["lam"][:].rearrange("p (a b) d -> p a b d", b=2)
                dve.wait_ge(*ctx_in.at(l, 64))
                done(v.tensor_tensor(lam[:, :, 0, :], lam[:, :, 0, :], lam[:, :, 1, :], ALU.mult), setup_v)
                done(v.tensor_reduce(m["lam2"][:, 0:2], lam[:, :, 0, :], AX_X, ALU.add), setup_v)
                taps(12)

                f0, f1 = (m[f][:].rearrange("p a b c d -> p (a b) (c d)") for f in ("fac0", "fac1"))
                dve.wait_ge(*z_done.at(l, 1))
                for i in range(4):
                    done(v.tensor_scalar(f1[:, i, :], ps[:, 4 + i, 0:T], column(R_BA + i), None, ALU.add), zb)
                dve.wait_ge(*setup_a.at(l, 1))
                lam2 = m["lam2"]
                done(v.tensor_tensor(lam2[:, 4:5], lam2[:, 2:3], lam2[:, 3:4], ALU.subtract), setup_v)
                done(v.tensor_scalar(lam2[:, 5:6], lam2[:, 4:5], m["lamc"][:, 0:1], -1.0, ALU.add, ALU.mult), setup_v)
                done(v.tensor_scalar(m["subg"][:], column(R_SUB), m["lamc"][:, 1:2], None, ALU.mult), setup_v)
                dve.wait_ge(*za.at(l, 3))
                done(v.scalar_tensor_tensor(f1, f1, 0.0, f0, ALU.min, ALU.subtract), decay)
                done(v.memset(m["prefix"][:, :, :, :, 0:1], 0.0), decay)
                for n in range(12):
                    d, ht, tt = n // 6, n // 3 % 2, n % 3
                    v.tensor_tensor_scan(m["prefix"][:, d, ht, tt, 1:P + 1], m["ones"][:], m["fac1"][:, d, ht, tt, :], 0.0,
                                         ALU.mult, ALU.add).then_inc(scan.sem, 1)
                dve.wait_ge(*scan.at(l, 12))

                fwd = m["prefix"][:, 0].rearrange("p a b t -> p (a b) t")
                bwd = m["prefix"][:, 1].rearrange("p a b t -> p (a b) t")

                def build(i):
                    f = m[f"fac{i % 2}"]
                    if i >= 2:
                        dve.wait_ge(*level_done.at(l, i))
                        dve.wait_ge(*copied.at(l, 3 * (i - 1)))
                    q, k = (f[:, s].rearrange("p a b t -> p (a b) t") for s in range(2))
                    if i < LEVELS:
                        n, g = 1 << i, 2 * NT

                        def halves(ap):
                            return ap.rearrange("p g (n s j) -> p g n s j", s=2, j=n)

                        def border(ap):
                            return halves(ap[:, :, 0:P])[:, :, :, 1, 0:1].broadcast_to([P, g, P // (2 * n), n])

                        incl, excl = halves(fwd[:, :, 1:P + 1]), halves(bwd[:, :, 0:P])
                        q, k = halves(q), halves(k)
                        v.tensor_tensor(q[:, :, :, 1, :], incl[:, :, :, 1, :], border(fwd), ALU.subtract).then_inc(built.sem, 1)
                        if i >= 2:
                            copy_level(i - 2)
                        v.tensor_tensor(k[:, :, :, 0, :], border(fwd), incl[:, :, :, 0, :], ALU.subtract).then_inc(built.sem, 1)
                        v.tensor_tensor(q[:, :, :, 0, :], border(bwd), excl[:, :, :, 0, :], ALU.subtract).then_inc(built.sem, 1)
                        v.tensor_tensor(k[:, :, :, 1, :], excl[:, :, :, 1, :], border(bwd), ALU.subtract).then_inc(built.sem, 1)
                    elif i == LEVELS:
                        total = fwd[:, :, P:P + 1].broadcast_to([P, 2 * NT, P])
                        v.tensor_copy(q, fwd[:, :, 1:P + 1]).then_inc(built.sem, 1)
                        copy_level(i - 2)
                        v.tensor_tensor(k, total, fwd[:, :, 1:P + 1], ALU.subtract).then_inc(built.sem, 1)
                    else:
                        total = bwd[:, :, P:P + 1].broadcast_to([P, 2 * NT, P])
                        v.tensor_tensor(q, total, bwd[:, :, 0:P], ALU.subtract).then_inc(built.sem, 1)
                        copy_level(i - 2)
                        v.tensor_copy(k, bwd[:, :, 0:P]).then_inc(built.sem, 1)

                def multiply(i):
                    f = m[f"fac{i % 2}"][:].rearrange("p a b c d -> p (a b c d)")
                    if i == 0:
                        dve.wait_ge(*pair_read[1].at(l, 4))
                        dve.wait_ge(*pair_read[0].at(l, 5))
                    dve.wait_ge(*expd.at(l, i + 1))
                    done(v.tensor_tensor(f, f, m["gqk"][:].rearrange("p a b t -> p (a b t)"), ALU.mult), factors)

                def copy_level(i):
                    for tt in range(NT):
                        src, dst = ps[:, 4 + tt, :].rearrange("p (a b) -> p a b", a=H), m["attn"][:, tt]
                        if i < 0:
                            dve.wait_ge(*level_done.at(l, 1))
                            v.tensor_copy(dst, src).then_inc(copied.sem, 1)
                        else:
                            mask = m["masks"][:, i:i + 1, :].broadcast_to([P, H, P])
                            v.copy_predicated(dst, mask, src).then_inc(copied.sem, 1)

                def rope(r):
                    side, ht = r // 2, 2 * (r % 2)
                    rot = ps[:, 7, :].rearrange("p (a b) -> p a b", a=2)
                    x = m["dqk"][:, side, ht:ht + 2, TP:T]
                    cos, sin = (m["rope"][:, i:i + 1, :].broadcast_to([P, 2, TS]) for i in range(2))
                    dve.wait_ge(*rot_done.at(l, r + 1))
                    done(v.tensor_tensor(rot, rot, sin, ALU.mult), roped)
                    done(v.tensor_tensor(x, x, cos, ALU.mult), roped)
                    done(v.tensor_tensor(x, x, rot, ALU.add), roped)

                build(0)
                build(1)
                copy_level(-1)
                multiply(0)
                multiply(1)
                for i in range(2, ROUNDS):
                    build(i)
                    taps(10)
                    multiply(i)
                    if i >= 5:
                        rope(i - 5)
                taps(TAPS * CT)
                def enter(d):
                    f, tt = m[f"fac{(LEVELS + d) % 2}"], 2 - d
                    dve.wait_ge(*etot_a.at(l, 2))
                    for ht in range(2):
                        done(v.tensor_scalar(m["q_enter"][:, d, ht, :], f[:, 0, ht, tt, :],
                                             m["etot"][:, 2 * d + ht:2 * d + ht + 1], None, ALU.mult), entered)

                def whole(d):
                    dve.wait_ge(*level_done.at(l, LEVELS + 2 + d))
                    done(v.tensor_copy(m["cross"][:, d], ps[:, 4 + d, :].rearrange("p (a b) -> p a b", a=H)), copied)
                    dve.wait_ge(*st_t.at(l, d + 1))
                    if d:
                        dve.wait_ge(*st_mm.at(l, 1))
                    done(v.tensor_copy(m["stateT"][:], ps[:, 6, 2 * d * P:2 * d * P + 2 * P]
                                       .rearrange("p (a b) -> p a b", a=2)), st_c)

                def state(d):
                    dve.wait_ge(*st_mm.at(l, d + 1))
                    if d:
                        dve.wait_ge(*st_out.at(l, 16))
                    done(v.tensor_copy(m["state_out"][:], ps[0:DK, 7, :].rearrange("p (a b) -> p a b", a=H)), st_v)

                for d in range(2):
                    enter(d)
                    whole(d)
                    state(d)
                for hh in range(H):
                    dve.wait_ge(*orstd.at(l, 2 * (hh + 1)))
                    done(v.scalar_tensor_tensor(m["rstd"][:], ps[:, 4 + hh % 2, 0:T], column(R_GN), m["rstd"][:], ALU.mult,
                                                ALU.mult), o_mul)
                    g = m["gg"][:, hh, :]
                    done(v.tensor_tensor(g, g, m["rstd"][:], ALU.mult), o_mul)
                dve.wait_ge(*mean_done.at(l, 1))
                for ct in range(CT):
                    a = m["conv_acc"][:, ct, :]
                    done(v.scalar_tensor_tensor(a, ps[:, 7, 0:AW], -1.0 / CONV, a, ALU.mult, ALU.add), centred)
                dve.wait_ge(*o_hi.at(l, 1))
                done(v.tensor_tensor(m["gla_lo"][:], m["gg"][:], m["gla_hi"][:].bitcast(F32), ALU.subtract), o_lo)

                def conv_norm():
                    dve.wait_ge(*crstd.at(l, 2))
                    r = m["t"][:].rearrange("p a b -> p (a b)")
                    for ct in range(CT):
                        for a, b, n in ((0, 0, TP), (A_S, TP, TS)):
                            done(v.scalar_tensor_tensor(m["conv_z"][:, ct, b:b + n], m["conv_acc"][:, ct, a:a + n],
                                                        column(R_LG + ct), r[:, a:a + n], ALU.mult, ALU.mult), conv_normed)

                def attention_gain(hh):
                    dve.wait_ge(*orstd.at(l, 2 * (H + hh + 1)))
                    g = m["gg"][:, hh, :]
                    done(v.scalar_tensor_tensor(g, g, m["subg"][:], m["rstd"][:], ALU.mult, ALU.mult), o_mul)

                mx = m["mx"]
                for u, (hh, q) in enumerate(UNITS):
                    n = keys_of(q)
                    dve.wait_ge(*sc_done.at(l, u + 1))
                    done(v.tensor_reduce(mx[:, 0:2], ps[:, 4:6, 0:n], AX_X, ALU.max), mx_v)
                    done(v.tensor_scalar(mx[:, 2:4], mx[:, 0:2], -DK ** -0.5, None, ALU.mult), mx_v)
                    dve.wait_ge(*ex_a.at(l, 2 * (u + 1)))
                    done(v.reciprocal(mx[:, 6:8], mx[:, 4:6]), w_v)
                    done(v.tensor_scalar(mx[:, 7:8], mx[:, 7:8], lam2[:, 5:6], None, ALU.mult), w_v)
                    p1, p2 = m["prob"][:, 0, 0:n], m["prob"][:, 1, 0:n]
                    done(v.tensor_scalar(p1, p1, mx[:, 6:7], None, ALU.mult), w_v)
                    done(v.scalar_tensor_tensor(p1, p2, mx[:, 7:8], p1, ALU.mult, ALU.add), w_v)
                    if u == 1:
                        conv_norm()
                    if u in (7, 10):
                        attention_gain(u // 3 - 2)
                attention_gain(2)
                attention_gain(3)
                dve.wait_ge(*o_hi.at(l, 2))
                done(v.tensor_tensor(m["diff_lo"][:], m["gg"][:], m["diff_hi"][:].bitcast(F32), ALU.subtract), o_lo)
                for ct in range(CT):
                    dve.wait_ge(*conv_sig.at(l, ct + 1))
                    z = m["conv_z"][:, ct, :]
                    done(v.scalar_tensor_tensor(z, z, column(R_LB + ct), m["conv_s"][:, ct, :], ALU.add, ALU.mult), conv_out)
                dve.wait_ge(*conv_hi_a.at(l, 1))
                done(v.tensor_tensor(m["conv_lo"][:], m["conv_z"][:], m["conv_hi"][:].bitcast(F32), ALU.subtract), conv_lo_v)

                for n in range(N_BR):
                    mc, b = n // 3, (0, 2, 1)[n % 3]
                    g = m["gates"][:, KD * b + 2 * mc:KD * b + 2 * mc + 2, :]
                    dve.wait_ge(*piece_used.at(l, BR0 + n + 1))
                    dve.wait_ge(*gsig.at(l, n % 3 + 1))
                    done(v.tensor_tensor(g, g, pair[n % 4], ALU.mult), gated)
                    if n % 3:
                        a = m["gates"][:, 2 * mc:2 * mc + 2, :]
                        done(v.tensor_tensor(a, a, g, ALU.add), summed)
                    if n % 3 == 2:
                        dve.wait_ge(*merged_a.at(l, mc + 1))
                        hi = m["h_hi"][:, 2 * mc:2 * mc + 2, :].bitcast(F32)
                        done(v.tensor_tensor(m["h_lo"][:, 2 * mc:2 * mc + 2, :], a, hi, ALU.subtract), merged_v)
                for cc in range(4):
                    dve.wait_ge(*piece_used.at(l, WO0 + 2 * cc + 2))
                    for i in range(2):
                        add_to_x(2 * cc + i, pair[cc % 2][:, i, :], 16)
                modulated_norm(1)

                def mod_chunk(full, before):
                    for k in range(KD):
                        if k % 2 == 0:
                            dve.wait_ge(mod_full[k // 2].sem, full)
                        for j in range(2):
                            mod_mac_op(k, k, j, m["acc"][:, 0], before)

                def mod_copy(dst):
                    v.tensor_copy(dst, ps[:, 7, 0:8].rearrange("p (a b) -> p a b", b=2)).then_inc(mod_out.sem, 1)

                with dve.Fori(0, PAIRS) as i:
                    dve.get_value_cache().nocache = True
                    mod_chunk(l * mod_full[0].per + i * 16 + (mod_full[0].credit + 16),
                              l * mod_mac.per + i * 2 * KD + mod_mac.credit)
                    dve.wait_ge(silu_a.sem, l * PAIRS + (i + 2))
                    dve.wait_ge(piece_used.sem, l * PIECES + i * 4 + (FI0 + 4 + SPL))
                    v.tensor_tensor(m["sq"][:], m["sq"][:], pair[1], ALU.mult).then_inc(u_v.sem, 1)
                    dve.wait_ge(uhi_a.sem, l * PAIRS + (i + 1))
                    v.tensor_tensor(m["act_lo"][:, bass.ds(i * 2, 2), :], m["sq"][:],
                                    m["act_hi"][:, bass.ds(i * 2, 2), :].bitcast(F32), ALU.subtract).then_inc(ulo_v.sem, 1)
                    dve.wait_ge(mod_red.sem, l * MOD_CHUNKS + i + (mod_red.credit + 1))
                    mod_copy(m["mod_sum"][:, bass.ds(i * 4, 4), :])
                mod_chunk(l * mod_full[0].per + (mod_full[0].credit + 16 * MOD_CHUNKS), l * mod_mac.per
                          + (mod_mac.credit + 2 * KD * PAIRS))
                dve.wait_ge(*mod_red.at(l, MOD_CHUNKS))
                mod_copy(m["mod_sum"][:, 4 * PAIRS:, :])
                for g in range(2):
                    dve.wait_ge(*piece_used.at(l, FO0 + 11 * (g + 1)))
                    for i in range(4):
                        add_to_x(4 * g + i, ps[:, 4 * g + i, 0:T], 40)

            dve.wait_ge(fin_a.sem, 2)
            for k in range(KD):
                v.scalar_tensor_tensor(m["x"][:, k, :], m["x"][:, k, :], m["prm"][:, R_FN + k:R_FN + k + 1], m["rstd"][:],
                                       ALU.mult, ALU.mult).then_inc(fin_v.sem, 1)
            for tt in range(NT):
                dve.wait_ge(fin_p.sem, tt + 1)
                v.tensor_copy(m["stage"][:, tt, :], flat[(0, 1, 3)[tt]]).then_inc(fin_v.sem, 1)


_INS = ['x_prompt', 'x_sample', 'cache_diff_k', 'cache_diff_v', 'state_gla', 'c', 'c_ctx', 'w_mod', 'b_mod', 'norm1_g',
        'norm2_g', 'w_in', 'gla_w_a2', 'gla_b_a', 'gla_norm_g', 'conv_w', 'conv_b', 'conv_ln_g', 'conv_ln_b',
        'diff_lambda', 'diff_subln_g', 'w_branch', 'w_out', 'w_ffn_in', 'w_ffn_out', 'final_norm_g']
_OUTS = [((1, TP, D), 'float32'), ((1, TS, D), 'float32'), ((1, DEPTH, TP, H, 2, DK), 'float32'),
         ((1, DEPTH, TP, H, DV), 'float32'), ((1, DEPTH, 2, H, DK, DV), 'float32')]


def _constants():
    import numpy as np
    grid_w, freqs, base = 64, 16, 10000.0
    inv = np.float32(base) ** (-np.arange(freqs, dtype=np.float32) / np.float32(freqs))
    tok = np.arange(TS)
    ang = np.stack([(tok // grid_w).astype(np.float32)[:, None] * inv, (tok % grid_w).astype(np.float32)[:, None] * inv], 1)
    p = np.arange(P)
    a = ang[:, p // 32 % 2, p % 16].T.astype(np.float32)
    rope = np.stack([np.cos(a), np.sin(a)], 1).astype(np.float32)
    swap = np.zeros((P, P), np.float32)
    for i in range(P):
        if i // 16 % 2 == 0:
            swap[i + 16, i] = -1.0
        else:
            swap[i - 16, i] = 1.0
    masks = np.zeros((P, LEVELS, P), np.float32)
    for n in range(LEVELS):
        h = 1 << n
        same = (p[:, None] // (2 * h)) == (p[None, :] // (2 * h))
        masks[:, n, :] = same & ((p[:, None] // h) != (p[None, :] // h))
    lam = np.array([[0.8 - 0.6 * math.exp(-0.3 * n), 1.0 - (0.8 - 0.6 * math.exp(-0.3 * n))] for n in range(DEPTH)],
                   np.float32)
    return {'k_rope': rope, 'k_swap': swap, 'k_ident': np.eye(P, dtype=np.float32), 'k_masks': masks, 'k_lam': lam}


def kernel(**inputs):
    import numpy as _np
    import concourse.bacc as _bacc
    from concourse import mybir as _mybir
    from concourse.bass_utils import run_bass_kernel_spmd as _run

    nc = _bacc.Bacc("TRN2", target_bir_lowering=False, num_devices=1)
    arrays, args = {}, []
    for name, a in [(n, inputs[n]) for n in _INS] + list(_constants().items()):
        a = _np.ascontiguousarray(a)
        arrays[f"in_{name}_dram"] = a
        args.append(nc.dram_tensor(f"in_{name}_dram", a.shape, _mybir.dt.from_np(a.dtype), kind="ExternalInput").ap())
    for i, (shape, dtype) in enumerate(_OUTS):
        dt = _mybir.dt.from_np(_np.dtype(dtype))
        args.append(nc.dram_tensor(f"out_{i}_dram", shape, dt, kind="ExternalOutput").ap())
    program(nc, *args)
    r = _run(nc, [arrays], core_ids=[0])
    return tuple(r.results[0][f"out_{i}_dram"] for i in range(len(_OUTS)))
```

```python
from contextlib import ExitStack
import math

import concourse.bass as bass
from concourse import mybir

F32 = mybir.dt.float32
F32R = mybir.dt.float32r
U8 = mybir.dt.uint8
ALU = mybir.AluOpType
ACT = mybir.ActivationFunctionType
AX_X = mybir.AxisListType.X

P = 128
D = 1024
KD = D // P
DEPTH = 2
TP, TS = 128, 256
T = TP + TS
NT = T // P
H = 4
DK = 64
DV = 128
RANK = 16
CONV = 512
CT = CONV // P
TAPS = 31
PAD = TAPS // 2
HID = 2816
KH = HID // P
EPS = 1e-6

C_GQ, C_GK, C_GV, C_GG, C_LR, C_CA, C_CG, C_DQ, C_DK, C_DV, C_GATE = (
    0, 256, 512, 1024, 1536, 1568, 2080, 2592, 3104, 3616, 4128)

YW = PAD + TP + PAD + TS + PAD
AW = TP + PAD + TS
Y_P, Y_S = PAD, PAD + TP + PAD
A_S = TP + PAD

RAW, SPL = 2, 4
IN_CHUNKS = ([(C_CG, 256), (C_CA, 256), (C_CG + 256, 256), (C_CA + 256, 256), (C_GG, 256), (C_GG + 256, 256),
              (C_LR, 2 * RANK), (C_GQ, 256), (C_GK, 256), (C_GV, 256), (C_GV + 256, 256),
              (C_DQ, 256), (C_DQ + 256, 256), (C_DK, 256), (C_DK + 256, 256), (C_DV, 256), (C_DV + 256, 256)]
             + [(C_GATE + 256 * i, 256) for i in range(12)])
N_IN = 2 * len(IN_CHUNKS)
N_BR = 12
BRANCHES = ((0, 0), (1, 0), (2, 0), (0, 2), (0, 1), (1, 2), (1, 1), (2, 2), (2, 1), (3, 0), (3, 2), (3, 1))
N_WO = 8
OUT_ORDER = ((0, 0), (1, 0), (0, 1), (1, 1), (2, 0), (2, 1), (3, 0), (3, 1))
PAIRS = KH // 2
N_FI = 4 * PAIRS
N_FO = KH
BR0, WO0, FI0, FO0 = N_IN, N_IN + N_BR, N_IN + N_BR + N_WO, N_IN + N_BR + N_WO + N_FI
PIECES = FO0 + N_FO
assert PIECES % SPL == 0 and PIECES % RAW == 0

MODR, ACCS = 4, 3
MOD_CHUNKS = 6 * D // 512
MOD_DVE = 2 * (KD - 4)
assert MOD_CHUNKS == PAIRS + 1

LEVELS = 7
ROUNDS = LEVELS + 2
UNITS = [(h, q) for h in range(H) for q in range(NT)]

LN_EXP = "natural_log_exp_and_others"

R_BMOD, R_N1, R_N2, R_BA, R_GN, R_CB, R_LG, R_LB, R_SUB, R_FN, R_END = (
    0, 48, 56, 64, 68, 69, 73, 77, 81, 82, 90)


class Signal:

    def __init__(self, nc, ctx, name, per=1, credit=0):
        self.sem = ctx.enter_context(nc.semaphore(name))
        self.per, self.credit, self.seen = per, credit, 0

    def at(self, layer, n):
        assert n + self.credit >= 1, n
        return self.sem, layer * self.per + (n + self.credit)

    def next(self):
        self.seen = self.seen % self.per + 1
        return self.seen


def memory(nc):
    m = {}
    top = [16512]

    def own(name, shape, dt=F32, size=None):
        n = size or math.prod(shape[1:]) * (1 if dt == U8 else 4)
        m[name] = nc.alloc_sbuf_tensor_at(name, shape, dt, offset=top[0])
        at = top[0]
        top[0] += (n + 31) // 32 * 32
        return at

    def over(name, shape, offset, dt=F32):
        m[name] = nc.alloc_sbuf_tensor_at(name, shape, dt, offset=offset)

    own("x", [P, KD, T])
    own("h_hi", [P, KD, T], F32R)
    own("h_lo", [P, KD, T], F32R)
    own("w_raw", [P, RAW, 1024])
    own("w_hi", [P, SPL, 1024], F32R)
    own("w_lo", [P, SPL, 1024], F32R)
    own("k_rows", [P, 512])
    gates = own("gates", [P, 24, T])
    gla = own("gla_hi", [P, H, T], F32R)
    own("gla_lo", [P, H, T], F32R)
    conv = own("conv_hi", [P, CT, T], F32R)
    conv_lo = own("conv_lo", [P, CT, T], F32R)
    diff = own("diff_hi", [P, H, T], F32R)
    diff_lo = own("diff_lo", [P, H, T], F32R)
    over("act_hi", [P, KH, T], gates, F32R)
    over("act_lo", [P, KH, T], gates + KH * T * 4, F32R)
    over("stage", [P, NT, D], gates)
    over("masks_in", [P, LEVELS, P], gates + NT * D * 4)
    over("conv_in", [P, CT, YW], gates + 15 * T * 4)
    over("conv_acc", [P, CT, AW], gates + 15 * T * 4 + (CT * YW * 4 + 31) // 32 * 32)
    assert CT * (YW + AW) + 8 <= 9 * T
    over("fac0", [P, 2, 2, NT, P], gla)
    over("gqk", [P, 2, 2, T], gla + 2 * 2 * T * 4)
    over("fac1", [P, 2, 2, NT, P], diff)
    over("gv", [P, NT, 512], diff_lo)
    over("attn", [P, NT, H, P], conv)
    over("cross", [P, 2, H, P], conv_lo)
    over("state0", [P, 2, 2, P], conv_lo + 2 * H * P * 4)
    over("conv_z", [P, CT, T], conv_lo)
    over("conv_s", [P, CT, T], conv)
    prefix = own("prefix", [P, 2, 2, NT, P + 1])
    over("prob", [P, 2, T], prefix)
    over("probT", [P, 2, NT, P], prefix + 2 * T * 4)
    gg = own("gg", [P, H, T])
    own("dqk", [P, 2, H, T])
    dv = own("dv", [P, NT, 512])
    over("ck_rows", [P, 512], dv)
    own("cv", [P, 512])
    own("ckT", [P, H, P])
    over("mod_w", [P, MODR, 2, 512], gg)
    over("mod_w_odd", [P, MODR, 2, 512], gla)
    over("mod_prod", [P, 2, 2, 2, 512], gla + MODR * 4096)
    assert (MODR + 4) * 4096 <= 3 * 2 * H * T * 4
    over("acc", [P, ACCS, 2, 512], gg + MODR * 4096)
    assert (MODR + ACCS) * 4096 <= (H + 2 * H) * T * 4 + NT * 512 * 4 + 2 * 512 * 4
    sq = own("sq", [P, 2, T])
    over("stateT", [P, 2, P], sq)
    over("state_out", [DK, H, P], sq + 2 * P * 4)
    t = own("t", [P, 2, T])
    over("lrT", [2 * RANK, T], t)
    over("q_enter", [P, 2, 2, P], t)
    own("rstd", [P, T])
    own("rope", [P, 2, TS])
    own("swap", [P, P])
    own("ident", [P, P])
    own("ones", [P, P])
    own("masks", [P, LEVELS, P], U8)
    own("wa", [2 * RANK, 2, 256])
    own("rows", [P, 2, P])
    own("prm", [P, R_END])
    own("cw", [P, TAPS * CT])
    own("csil", [P, 16])
    own("mod_sum", [P, 48, 2])
    own("mod", [P, 48, 2])
    own("eff", [P, 2, KD, 2])
    own("lam", [P, 4, DK])
    own("lam2", [P, 8])
    own("lamc", [P, 2])
    own("subg", [P, 1])
    own("eps", [P, 1])
    own("one", [P, 1])
    own("mx", [P, 8])
    own("etot", [P, 4])
    assert top[0] <= nc.sbuf_usable_end, (top[0], nc.sbuf_usable_end)
    return m


def program(nc, x_prompt, x_sample, cache_diff_k, cache_diff_v, state_gla, c, c_ctx, w_mod, b_mod, norm1_g, norm2_g,
            w_in, gla_w_a2, gla_b_a, gla_norm_g, conv_w, conv_b, conv_ln_g, conv_ln_b, diff_lambda, diff_subln_g,
            w_branch, w_out, w_ffn_in, w_ffn_out, final_norm_g, k_rope, k_swap, k_ident, k_masks, k_lam,
            y_prompt, y_sample, new_k, new_v, new_s):
    with ExitStack() as ctx:
        m = memory(nc)
        ps = ctx.enter_context(nc.psum_tensor("ps", [P, 8, 512], F32))
        pair = [ps[:, 2 * i:2 * i + 2, 0:T] for i in range(4)]
        flat = [ps[:, 2 * i:2 * i + 2, :].rearrange("p a b -> p (a b)") for i in range(4)]

        def signal(name, per=1, credit=0):
            return Signal(nc, ctx, name, per, credit)

        raw_full = [signal(f"raw_full{i}", 16 * PIECES // RAW) for i in range(RAW)]
        hi_ready = signal("hi_ready", PIECES, RAW)
        lo_ready = signal("lo_ready", PIECES, RAW)
        piece_used = signal("piece_used", PIECES, SPL)
        mod_full = [signal(f"mod_full{i}", 16 * MOD_CHUNKS, 16 * MOD_CHUNKS // 2) for i in range(MODR)]
        mod_mac = signal("mod_mac", 2 * KD * MOD_CHUNKS, MOD_DVE * MOD_CHUNKS)
        mod_full_odd = [signal(f"mod_full_odd{i}") for i in range(MODR)]
        mod_part = signal("mod_part")
        mod_first = signal("mod_first")
        mod_prod = signal("mod_prod")
        mod_pool = signal("mod_pool")
        mod_red = signal("mod_red", MOD_CHUNKS, MOD_CHUNKS)
        mod_out = signal("mod_out", MOD_CHUNKS, MOD_CHUNKS)
        const_in = signal("const_in")
        first_in = signal("first_in")
        start_v = signal("start_v")
        masks_v = signal("masks_v")
        start_a = signal("start_a")
        start_p = signal("start_p")
        rows_in = signal("rows_in", 16 * 11)
        wa_in = signal("wa_in", 32)
        ctx_in = signal("ctx_in", 16 * 4)
        state_in = signal("state_in", 16 * 4)
        rows_t = signal("rows_t", 1, 1)
        keys_t = signal("keys_t")
        small_v = signal("small_v", 3)
        setup_v = signal("setup_v", 8, 1)
        setup_a = signal("setup_a")
        x_part = signal("x_part", 2 * KD)
        x_ready = signal("x_ready", 2 * KD)
        sq_ready = signal("sq_ready", 2 * KD, KD)
        sq_used = signal("sq_used", 2 * KD, KD)
        rstd_a = signal("rstd_a", 4)
        t_ready = signal("t_ready", 4 * KD)
        h_hi_ready = signal("h_hi_ready", 4 * KD)
        h_lo_ready = signal("h_lo_ready", 4 * KD)
        pair_read = [signal("pair_read0", 15), signal("pair_read1", 14)]
        gg_sig = signal("gg_sig", 2)
        pads = signal("pads", 3)
        y_prompt_ready = signal("y_prompt_ready", 2)
        tap = signal("tap", TAPS * CT)
        mean_done = signal("mean_done")
        centred = signal("centred", CT)
        csq = signal("csq", CT)
        csq_used = signal("csq_used", CT)
        crstd = signal("crstd", 2)
        conv_normed = signal("conv_normed", 2 * CT)
        conv_sig = signal("conv_sig", CT)
        conv_out = signal("conv_out", CT)
        conv_hi_a = signal("conv_hi_a")
        conv_lo_v = signal("conv_lo_v")
        z_done = signal("z_done", 1, 1)
        zb = signal("zb", 4)
        za = signal("za", 3)
        decay = signal("decay", 2)
        scan = signal("scan", 12)
        etot_a = signal("etot_a", 2)
        built = signal("built", 4 * LEVELS + 4)
        expd = signal("expd", ROUNDS)
        factors = signal("factors", ROUNDS)
        level_done = signal("level_done", ROUNDS + 1)
        even_heads = signal("even_heads", ROUNDS + 1)
        copied = signal("copied", 3 * (LEVELS + 1) + 2)
        entered = signal("entered", 4)
        st_t = signal("st_t", 2)
        st_c = signal("st_c", 2)
        st_mm = signal("st_mm", 2)
        st_v = signal("st_v", 2)
        st_out = signal("st_out", 32)
        o_done = signal("o_done", H)
        osq = signal("osq", 2 * H)
        oss = signal("oss", 2 * H)
        orstd = signal("orstd", 4 * H)
        o_mul = signal("o_mul", 3 * H)
        o_copy = signal("o_copy", H)
        o_hi = signal("o_hi", 2)
        o_lo = signal("o_lo", 2)
        rot_done = signal("rot_done", 4)
        roped = signal("roped", 12)
        kT_done = signal("kT_done")
        k_rows = signal("k_rows")
        kv_out = signal("kv_out", 32, 1)
        sc_done = signal("sc_done", 12)
        mx_v = signal("mx_v", 24)
        ex_a = signal("ex_a", 24)
        w_v = signal("w_v", 48)
        tp_done = signal("tp_done", 12)
        wt_a = signal("wt_a", 12)
        pv_done = signal("pv_done", 12, 1)
        gsig = signal("gsig", 4)
        gated = signal("gated", N_BR)
        summed = signal("summed", 8)
        merged_a = signal("merged_a", 4)
        merged_v = signal("merged_v", 4)
        tile_done = signal("tile_done", 10)
        silu_a = signal("silu_a", PAIRS, 1)
        u_v = signal("u_v", PAIRS, 1)
        uhi_a = signal("uhi_a", PAIRS)
        ulo_v = signal("ulo_v", PAIRS, 1)
        fin_a = signal("fin_a")
        fin_v = signal("fin_v")
        fin_p = signal("fin_p")
        y_out = signal("y_out")

        def keys_of(q):
            return P if q == 0 else T

        def first_mod(c, j):
            if c % 2:
                return m["mod_w_odd"][:, j], (mod_full_odd[j].sem, 16 * (c // 2 + 1))
            return m["mod_w"][:, j], (mod_full[j].sem, 16 * (c // 2 + 1))

        block = ctx.enter_context(nc.Block())

        @block.sync
        def _(sp):
            sp.sem_inc(kv_out.sem, 1)
            for src, dst in ((k_ident, "ident"), (k_rope, "rope"), (k_swap, "swap"), (k_masks, "masks_in")):
                sp.dma_start(m[dst][:], src).then_inc(const_in.sem, 16)
            sp.dma_start(m["rows"][0:8, 0, :], c_ctx.rearrange("(k p) -> k p", p=P)).then_inc(first_in.sem, 16)
            sp.dma_start(m["rows"][8:16, 0, :], c.rearrange("b (k p) -> (b k) p", p=P)).then_inc(first_in.sem, 16)
            sp.dma_start(m["stage"][:, 0, :], x_prompt[0]).then_inc(first_in.sem, 16)
            sp.dma_start(m["stage"][:, 1:3, :], x_sample[0].rearrange("(t p) d -> p t d", p=P)).then_inc(first_in.sem, 16)

            def mod_piece(layer, col, j, to=None, full=None):
                sp.dma_start(to or m["mod_w"][:, j],
                             w_mod[layer, 256 * j:256 * j + 256, col].rearrange("(k p) n -> p k n", p=P)
                             ).then_inc(full or mod_full[j].sem, 16)

            for n in range(MOD_CHUNKS):
                for j in range(MODR):
                    if n >= 2:
                        if j == 0:
                            sp.wait_ge(mod_part.sem, n - 1)
                            sp.wait_ge(mod_first.sem, 2 * (n - 1))
                        elif j == 1:
                            sp.wait_ge(mod_prod.sem, 4 * (n - 1))
                        else:
                            sp.wait_ge(mod_mac.sem, MOD_DVE * (n - 2) + 4 * (j - 1))
                    to, full = first_mod(n, j)
                    mod_piece(0, slice(512 * n, 512 * n + 512), j, to, full[0])

            with sp.Fori(0, DEPTH) as l:
                sp.get_value_cache().nocache = True

                def piece(s, src):
                    sp.wait_ge(*hi_ready.at(l, s - RAW + 1))
                    sp.wait_ge(*lo_ready.at(l, s - RAW + 1))
                    k, n = src.shape[0] // P, src.shape[1]
                    sp.dma_start(m["w_raw"][:, s % RAW, 0:k * n].rearrange("p (k n) -> p k n", k=k),
                                 src.rearrange("(k p) n -> p k n", p=P)).then_inc(raw_full[s % RAW].sem, 16)

                sp.wait_ge(start_p.sem, 1)
                sp.wait_ge(*rows_t.at(l, 0))
                row = 0
                for src in (b_mod[l].rearrange("(r p) -> r p", p=P), norm1_g[l].rearrange("(r p) -> r p", p=P),
                            norm2_g[l].rearrange("(r p) -> r p", p=P),
                            gla_b_a[l].rearrange("d (r p) -> (d r) p", p=P), gla_norm_g[l].rearrange("(r p) -> r p", p=P),
                            conv_b[l].rearrange("(r p) -> r p", p=P), conv_ln_g[l].rearrange("(r p) -> r p", p=P),
                            conv_ln_b[l].rearrange("(r p) -> r p", p=P), diff_subln_g[l].rearrange("(r p) -> r p", p=P),
                            final_norm_g.rearrange("(r p) -> r p", p=P)):
                    sp.dma_start(m["rows"][row:row + src.shape[0], 0, :], src).then_inc(rows_in.sem, 16)
                    row += src.shape[0]
                assert row == R_END
                sp.dma_start(m["rows"][0:TAPS * CT, 1, :], conv_w[l].rearrange("w (r p) -> (w r) p", p=P)
                             ).then_inc(rows_in.sem, 16)
                for s in range(N_IN):
                    col, width = IN_CHUNKS[s // 2]
                    half = s % 2
                    piece(s, w_in[l, half * 512:(half + 1) * 512, col:col + width])
                    if s == 2:
                        sp.wait_ge(start_v.sem, 4)
                        sp.wait_ge(*z_done.at(l, 0))
                        sp.dma_start(m["wa"][0:RANK, 0, :], gla_w_a2[l, 0]).then_inc(wa_in.sem, 16)
                        sp.dma_start(m["wa"][RANK:2 * RANK, 1, :], gla_w_a2[l, 1]).then_inc(wa_in.sem, 16)
                        sp.wait_ge(*mod_red.at(l, 0))
                        sp.dma_start(m["ck_rows"][:], cache_diff_k[0, l].rearrange("t h j d -> t (h j d)")
                                     ).then_inc(ctx_in.sem, 16)
                        sp.dma_start(m["cv"][:], cache_diff_v[0, l].rearrange("t h d -> t (h d)")).then_inc(ctx_in.sem, 16)
                        sp.wait_ge(*setup_v.at(l, 0))
                        sp.dma_start(m["lam"][:], diff_lambda[l].partition_broadcast(P)).then_inc(ctx_in.sem, 16)
                        sp.dma_start(m["lamc"][:], k_lam[l].partition_broadcast(P)).then_inc(ctx_in.sem, 16)
                    if s == 6:
                        sp.wait_ge(*x_ready.at(l, KD))
                        for d in range(2):
                            for hh in range(2):
                                sp.dma_start(m["state0"][DK * hh:DK * hh + DK, d, :, :],
                                             state_gla[0, l, d].rearrange("(t s) k v -> s k t v", s=2)[hh]
                                             ).then_inc(state_in.sem, 16)
                    if s == 39:
                        sp.wait_ge(*pair_read[0].at(l, 9))
                        sp.wait_ge(*pair_read[1].at(l, 8))
                        sp.dma_start(new_v[0, l].rearrange("t h d -> t (h d)"), m["dv"][:, 0, :]).then_inc(kv_out.sem, 16)
                    if s == 42:
                        sp.wait_ge(*k_rows.at(l, 1))
                        sp.dma_start(new_k[0, l].rearrange("t h j d -> t (h j d)"), m["k_rows"][:]
                                     ).then_inc(kv_out.sem, 16)
                    if s in (45, 47):
                        d = (s - 45) // 2
                        sp.wait_ge(*st_v.at(l, d + 1))
                        sp.dma_start(new_s[0, l, d].rearrange("h k v -> k h v"), m["state_out"][:]).then_inc(st_out.sem, 16)
                for n in range(N_BR):
                    mc, b = BRANCHES[n]
                    piece(BR0 + n, w_branch[l, b * 512:(b + 1) * 512, 256 * mc:256 * mc + 256])
                sp.wait_ge(*pv_done.at(l, 12))
                sp.wait_ge(*o_lo.at(l, 2))
                sp.wait_ge(*kv_out.at(l, 32))
                for s in range(N_WO):
                    cc, half = OUT_ORDER[s]
                    piece(WO0 + s, w_out[l, half * 512:(half + 1) * 512, 256 * cc:256 * cc + 256])
                following = (l + 1) % DEPTH
                with sp.Fori(0, PAIRS) as i:
                    sp.get_value_cache().nocache = True
                    for j in range(4):
                        half, part = j % 2, j // 2
                        s = FI0 + j
                        sp.wait_ge(hi_ready.sem, l * PIECES + i * 4 + (s + 1))
                        sp.wait_ge(lo_ready.sem, l * PIECES + i * 4 + (s + 1))
                        sp.dma_start(m["w_raw"][:, s % RAW, :].rearrange("p (k n) -> p k n", k=4),
                                     w_ffn_in[l, half * 512:(half + 1) * 512, bass.ds(i * 256 + part * HID, 256)]
                                     .rearrange("(k p) n -> p k n", p=P)).then_inc(raw_full[s % RAW].sem, 16)
                        sp.wait_ge(mod_mac.sem, l * mod_mac.per + i * 2 * KD + (mod_mac.credit - 2 * KD + 4 * (j + 1)))
                        mod_piece(following, bass.ds(i * 512, 512), j)
                for s in range(N_FO):
                    g, kk = s // 11, s % 11
                    piece(FO0 + s, w_ffn_out[l, kk * 256:(kk + 1) * 256, 512 * g:512 * g + 512])
                    if s < MODR:
                        sp.wait_ge(*mod_mac.at(l, 2 * KD * (PAIRS - 1) + 4 * (s + 1)))
                        mod_piece(following, slice(512 * PAIRS, 512 * PAIRS + 512), s)
            for half in range(2):
                for tt in range(NT):
                    sp.wait_ge(fin_v.sem, KD + NT * half + tt + 1)
                    dst = y_prompt[0] if tt == 0 else y_sample[0, (tt - 1) * P:tt * P]
                    sp.dma_start(dst[:, 512 * half:512 * half + 512], m["stage"][:, tt, 512 * half:512 * half + 512]
                                 ).then_inc(y_out.sem, 16)
            sp.wait_ge(*kv_out.at(DEPTH, 0))
            sp.wait_ge(st_out.sem, 32 * DEPTH)
            sp.wait_ge(y_out.sem, 32 * NT)

        @block.gpsimd
        def _(pool):
            pool.sem_inc(lo_ready.sem, RAW)
            for c in range(MOD_CHUNKS):
                for k in (2, 3):
                    for j in range(2):
                        pool.wait_ge(mod_prod.sem, 4 * c + 2 * (k - 2) + j + 1)
                        if k == 2:
                            pool.wait_ge(mod_first.sem, 2 * c + j + 1)
                        else:
                            pool.wait_ge(mod_pool.sem, 4 * c + j + 1)
                        a = m["acc"][:, c % ACCS, j, :]
                        nc.gpsimd.tensor_tensor(a, a, m["mod_prod"][:, c % 2, k - 2, j, :], ALU.add
                                                ).then_inc(mod_pool.sem, 1)
            with pool.Fori(0, DEPTH * PIECES // 4) as g:
                pool.get_value_cache().nocache = True
                for j in range(4):
                    pool.wait_ge(raw_full[j % RAW].sem, g * (16 * 4 // RAW) + 16 * (j // RAW + 1))
                    pool.wait_ge(hi_ready.sem, g * 4 + (j + 1 + RAW))
                    nc.gpsimd.tensor_tensor(m["w_lo"][:, j], m["w_raw"][:, j % RAW], m["w_hi"][:, j].bitcast(F32),
                                            ALU.subtract).then_inc(lo_ready.sem, 1)

        @block.tensor
        def _(pe):
            mm = nc.tensor.matmul
            ident, ones = m["ident"], m["ones"]
            pe.sem_inc(piece_used.sem, SPL)
            pe.sem_inc(rows_t.sem, 1)
            pe.sem_inc(z_done.sem, 1)
            pe.sem_inc(pv_done.sem, 1)
            pe.wait_ge(const_in.sem, 64)
            pe.wait_ge(first_in.sem, 64)
            nc.tensor.transpose(ps[:, 7, T:T + 16], m["rows"][0:16, 0, :], ident[0:16, 0:16]).then_inc(start_p.sem, 1)
            for k in range(KD):
                if k == 7:
                    pe.wait_ge(start_v.sem, 5)
                for tt in range(NT):
                    ins = nc.tensor.transpose(ps[:, k, tt * P:tt * P + P], m["stage"][:, tt, k * P:k * P + P], ident[:])
                ins.then_inc(start_p.sem, 1)

            cond = m["csil"][:].rearrange("p (j k) -> p k j", k=KD)

            def mod_sums(bank, acc, start):
                for t4 in range(4):
                    for j in range(2):
                        ins = mm(ps[:, bank, 2 * t4 + j:2 * t4 + j + 1], acc[:, j, P * t4:P * t4 + P], ones[:, 0:1],
                                 start=start, stop=True, skip_group_check=True)
                ins.then_inc(mod_red.sem, 1)

            def square_sum(layer, norm, k):
                pe.wait_ge(*sq_ready.at(layer, k + 1 if norm else k + 1 - KD))
                mm(ps[:, 4 * norm, 0:T], ones[:], m["sq"][:, k % 2, :], start=k == 0, stop=k == KD - 1
                   ).then_inc(sq_used.sem, 1)

            pe.wait_ge(x_ready.sem, KD)
            for c in range(MOD_CHUNKS + 1):
                if c in (5, 9):
                    square_sum(0, 0, c // 4 * 2 - 2)
                    square_sum(0, 0, c // 4 * 2 - 1)
                if c >= 4:
                    pe.wait_ge(mod_out.sem, c - 3)
                if c < MOD_CHUNKS:
                    w, full = first_mod(c, 0)
                    pe.wait_ge(*full)
                    for t4 in range(4):
                        ins = mm(ps[:, 4 + c % 4, 2 * t4:2 * t4 + 2], w[:, 0, P * t4:P * t4 + P],
                                 cond[:, 0, :], start=t4 == 0, stop=False, skip_group_check=True)
                    ins.then_inc(mod_part.sem, 1)
                if c:
                    pe.wait_ge(mod_mac.sem, MOD_DVE * c)
                    mod_sums(4 + (c - 1) % 4, m["acc"][:, (c - 1) % ACCS], False)

            with pe.Fori(0, DEPTH) as l:
                pe.get_value_cache().nocache = True

                def mix(s, lhs_j, outs, k, rhs, start, stop):
                    ins = None
                    hi, lo = m["w_hi"][:, s % SPL, :], m["w_lo"][:, s % SPL, :]
                    for out, at in zip(outs, lhs_j):
                        mm(out, hi[:, at:at + P], rhs[0][:, k, :], start=start, stop=False)
                        mm(out, hi[:, at:at + P], rhs[1][:, k, :], start=False, stop=False)
                        ins = mm(out, lo[:, at:at + P], rhs[0][:, k, :], start=False, stop=stop)
                    return ins

                def split(s):
                    pe.wait_ge(*hi_ready.at(l, s + 1))
                    pe.wait_ge(*lo_ready.at(l, s + 1))

                h = (m["h_hi"], m["h_lo"])

                pe.wait_ge(*rows_in.at(l, 16 * 11))
                pe.wait_ge(*x_ready.at(l, 2))
                nc.tensor.transpose(ps[:, 1, 0:R_END], m["rows"][0:R_END, 0, :], ident[0:R_END, 0:R_END])
                nc.tensor.transpose(ps[:, 1, P:P + TAPS * CT], m["rows"][0:TAPS * CT, 1, :],
                                    ident[0:TAPS * CT, 0:TAPS * CT]).then_inc(rows_t.sem, 1)
                for k in range(4, KD):
                    square_sum(l, 0, k)

                def chunk_piece(s):
                    c, half = s // 2, s % 2
                    col, width = IN_CHUNKS[c]
                    split(s)
                    if half == 0 and c >= 2:
                        pe.wait_ge(*pair_read[c % 2].at(l, c // 2))
                    out = pair[c % 2]
                    ins = None
                    if c == 6:
                        for j in range(4):
                            k = 4 * half + j
                            o = out[0:2 * RANK, 0, :]
                            w = [m[n][:, s % SPL, j * 32:j * 32 + 32] for n in ("w_hi", "w_lo")]
                            mm(o, w[0], h[0][:, k, :], start=k == 0, stop=False)
                            mm(o, w[0], h[1][:, k, :], start=False, stop=False)
                            ins = mm(o, w[1], h[0][:, k, :], start=False, stop=k == KD - 1)
                    elif col in (C_GV, C_GV + 256, C_DV, C_DV + 256):
                        for j in range(4):
                            k = 4 * half + j
                            w = [m[n][:, s % SPL, j * 256:j * 256 + 256] for n in ("w_hi", "w_lo")]
                            for tt in range(NT):
                                o = flat[c % 2][:, tt * 256:tt * 256 + 256]
                                x = [h[i][:, k, tt * P:tt * P + P] for i in range(2)]
                                mm(o, x[0], w[0], start=k == 0 and tt != 1, stop=False, skip_group_check=True)
                                mm(o, x[0], w[1], start=False, stop=False, skip_group_check=True)
                                ins = mm(o, x[1], w[0], start=False, stop=k == KD - 1, skip_group_check=True)
                    else:
                        for j in range(4):
                            k = 4 * half + j
                            if c == 0:
                                pe.wait_ge(*h_lo_ready.at(l, 2 * (k + 1)))
                            ins = mix(s, [j * 256, j * 256 + P], [out[:, 0, :], out[:, 1, :]], k, h, k == 0, k == KD - 1)
                    ins.then_inc(piece_used.sem, 1)

                def heads(bank):
                    return [ps[:, bank, P * hh:P * hh + P] for hh in range(H)]

                def part(name, side, hh, tt):
                    rows = slice(DK * (hh % 2), DK * (hh % 2) + DK)
                    x = m[name]
                    if name == "gqk":
                        return x[rows, side, hh // 2, tt * P:tt * P + P]
                    return x[rows, side, hh // 2, tt, :]

                def even_heads_done(ins, n):
                    ins.then_inc(even_heads.sem, 1)
                    pe.wait_ge(*even_heads.at(l, n))

                def level(i):
                    if i >= 0:
                        pe.wait_ge(*factors.at(l, i + 1))
                        pe.wait_ge(*copied.at(l, 3 * (i + 1)))
                    else:
                        pe.wait_ge(*zb.at(l, 4))
                        pe.wait_ge(*pair_read[1].at(l, 4))
                        pe.wait_ge(*pair_read[0].at(l, 5))
                    for odd in range(2):
                        for tt in range(NT):
                            for hh in (odd, odd + 2):
                                out = heads(4 + tt)[hh]
                                if i < 0:
                                    mm(out, part("gqk", 1, hh, tt), part("gqk", 0, hh, tt), start=True, stop=False)
                                    ins = mm(out, part("gqk", 1, hh, tt), part("gqk", 0, hh, tt), start=False, stop=True)
                                else:
                                    f = f"fac{i % 2}"
                                    ins = mm(out, part(f, 1, hh, tt), part(f, 0, hh, tt), start=True, stop=True)
                        if odd == 0:
                            even_heads_done(ins, i + 2)
                    ins.then_inc(level_done.sem, 1)

                def whole(d):
                    i = LEVELS + d
                    f, kt, qt = f"fac{i % 2}", 1 + d, 2 - d
                    pe.wait_ge(*factors.at(l, i + 1))
                    pe.wait_ge(*copied.at(l, 3 * (LEVELS + 1)))
                    for hh in (0, 2, 1, 3):
                        ins = mm(heads(4 + d)[hh], part(f, 1, hh, kt), part(f, 0, hh, qt), start=True, stop=True)
                        if hh == 2:
                            even_heads_done(ins, LEVELS + 2 + d)
                    ins.then_inc(level_done.sem, 1)
                    if d:
                        pe.wait_ge(*st_c.at(l, 1))
                    for ht in range(2):
                        ins = nc.tensor.transpose(ps[:, 6, (2 * d + ht) * P:(2 * d + ht) * P + P],
                                                  m[f][:, 1, ht, 0, :], ident[:])
                    ins.then_inc(st_t.sem, 1)

                def state(d):
                    pe.wait_ge(*st_c.at(l, d + 1))
                    pe.wait_ge(*pair_read[1].at(l, 5))
                    pe.wait_ge(*pair_read[0].at(l, 6))
                    pe.wait_ge(*k_rows.at(l, 1))
                    if d:
                        pe.wait_ge(*st_v.at(l, 1))
                    for hh in range(H):
                        lo = DK * (hh % 2)
                        ins = mm(ps[0:DK, 7, P * hh:P * hh + P], m["stateT"][:, hh // 2, lo:lo + DK],
                                 m["gv"][:, 0, P * hh:P * hh + P], start=True, stop=True)
                    ins.then_inc(st_mm.sem, 1)

                def gla_out(hh):
                    rows = slice(DK * (hh % 2), DK * (hh % 2) + DK)
                    cols = slice(P * hh, P * hh + P)
                    bank = 4 + hh % 2
                    if hh == 0:
                        pe.wait_ge(*copied.at(l, 3 * (LEVELS + 1) + 2))
                        pe.wait_ge(*entered.at(l, 4))
                        pe.wait_ge(*state_in.at(l, 64))
                    if hh >= 2:
                        pe.wait_ge(*o_mul.at(l, 2 * (hh - 1)))
                    v, att, cr, s0 = m["gv"], m["attn"], m["cross"], m["state0"]
                    mm(ps[:, bank, 0:P], v[:, 0, cols], att[:, 0, hh, :], start=True, stop=True)
                    o = ps[:, bank, P:2 * P]
                    mm(o, v[:, 1, cols], att[:, 1, hh, :], start=True, stop=False)
                    mm(o, v[:, 2, cols], cr[:, 1, hh, :], start=False, stop=False)
                    mm(o, s0[rows, 0, hh // 2, :], part("fac1", 0, hh, 1), start=False, stop=False)
                    mm(o, s0[rows, 1, hh // 2, :], m["q_enter"][rows, 1, hh // 2, :], start=False, stop=True)
                    o = ps[:, bank, 2 * P:3 * P]
                    mm(o, v[:, 2, cols], att[:, 2, hh, :], start=True, stop=False)
                    mm(o, v[:, 1, cols], cr[:, 0, hh, :], start=False, stop=False)
                    mm(o, s0[rows, 0, hh // 2, :], m["q_enter"][rows, 0, hh // 2, :], start=False, stop=False)
                    mm(o, s0[rows, 1, hh // 2, :], part("fac0", 0, hh, 2), start=False, stop=True).then_inc(o_done.sem, 1)

                def head_square_sum(n):
                    pe.wait_ge(*osq.at(l, n + 1))
                    if n == 0:
                        pe.wait_ge(*st_c.at(l, 2))
                    if n >= H:
                        pe.wait_ge(*wt_a.at(l, min(3 * (n - H) + 5, 12)))
                    mm(ps[:, 6, 0:T], ones[:], m["rstd"][:], start=True, stop=True).then_inc(oss.sem, 1)

                def rotate(r):
                    side, ht = r // 2, 2 * (r % 2)
                    pe.wait_ge(*pair_read[(11 + r) % 2].at(l, (11 + r) // 2 + 1))
                    if r == 0:
                        pe.wait_ge(*zb.at(l, 4))
                    else:
                        pe.wait_ge(*roped.at(l, 3 * r))
                    for j in range(2):
                        ins = mm(ps[:, 7, j * TS:j * TS + TS], m["swap"][:], m["dqk"][:, side, ht + j, TP:T],
                                 start=True, stop=True)
                    ins.then_inc(rot_done.sem, 1)

                def prompt_keys():
                    pe.wait_ge(*roped.at(l, 12))
                    for hh in range(H):
                        ins = nc.tensor.transpose(ps[:, 7, P * hh:P * hh + P], m["dqk"][:, 1, hh, 0:TP], ident[:])
                    ins.then_inc(kT_done.sem, 1)

                def scores(u):
                    hh, q = UNITS[u]
                    if u == 0:
                        pe.wait_ge(*o_mul.at(l, 2 * H))
                        pe.wait_ge(*small_v.at(l, 3))
                    else:
                        pe.wait_ge(*ex_a.at(l, 2 * u))
                    for t in range(2):
                        rows = slice(DK * t, DK * t + DK)
                        qT = m["dqk"][rows, 0, hh, P * q:P * q + P]
                        if q == 0:
                            ins = mm(ps[:, 4 + t, 0:P], qT, m["dqk"][rows, 1, hh, 0:P], start=True, stop=True)
                        else:
                            mm(ps[:, 4 + t, 0:TS], qT, m["dqk"][rows, 1, hh, TP:T], start=True, stop=True)
                            ins = mm(ps[:, 4 + t, TS:T], qT, m["ckT"][rows, hh, :], start=True, stop=True)
                    ins.then_inc(sc_done.sem, 1)

                def weights_T(u):
                    hh, q = UNITS[u]
                    pe.wait_ge(*w_v.at(l, 4 * (u + 1)))
                    if u == 0:
                        pe.wait_ge(*orstd.at(l, 2 * H))
                    else:
                        pe.wait_ge(*wt_a.at(l, u))
                    if u in (5, 8, 11):
                        pe.wait_ge(*orstd.at(l, 2 * (H + u // 3) - 1))
                    for kt in range(keys_of(q) // P):
                        ins = nc.tensor.transpose(ps[:, 6, P * kt:P * kt + P], m["prob"][:, 0, P * kt:P * kt + P], ident[:])
                    ins.then_inc(tp_done.sem, 1)

                def values(u):
                    hh, q = UNITS[u]
                    cols = slice(P * hh, P * hh + P)
                    pe.wait_ge(*wt_a.at(l, u + 1))
                    if u == 0:
                        pe.wait_ge(*crstd.at(l, 1))
                        pe.wait_ge(*pair_read[1].at(l, 8))
                        pe.wait_ge(*pair_read[0].at(l, 9))
                    elif q == 0:
                        pe.wait_ge(*o_copy.at(l, hh))
                    src = [m["dv"][:, 0, cols]] if q == 0 else [m["dv"][:, 1, cols], m["dv"][:, 2, cols], m["cv"][:, cols]]
                    for kt, v in enumerate(src):
                        ins = mm(ps[:, 7, P * q:P * q + P], v, m["probT"][:, u % 2, kt, :], start=kt == 0,
                                 stop=kt == len(src) - 1)
                    ins.then_inc(pv_done.sem, 1)

                def conv_mean():
                    pe.wait_ge(*tap.at(l, TAPS * CT))
                    pe.wait_ge(*st_v.at(l, 2))
                    for ct in range(CT):
                        ins = mm(ps[:, 7, 0:AW], ones[:], m["conv_acc"][:, ct, :], start=ct == 0, stop=ct == CT - 1)
                    ins.then_inc(mean_done.sem, 1)

                def conv_var():
                    pe.wait_ge(*centred.at(l, CT))
                    for ct in range(CT):
                        pe.wait_ge(*csq.at(l, ct + 1))
                        mm(ps[:, 7, 0:AW], ones[:], m["t"][:].rearrange("p a b -> p (a b)")[:, 0:AW], start=ct == 0,
                           stop=ct == CT - 1).then_inc(csq_used.sem, 1)

                for s in range(N_IN):
                    chunk_piece(s)
                    if s == 6:
                        pe.wait_ge(*ctx_in.at(l, 64))
                        for hh in range(H):
                            ins = nc.tensor.transpose(ps[:, 6, P * hh:P * hh + P], m["ck_rows"][:, P * hh:P * hh + P],
                                                      ident[:])
                        ins.then_inc(keys_t.sem, 1)
                    if s == 17:
                        pe.wait_ge(*pair_read[0].at(l, 4))
                        pe.wait_ge(*wa_in.at(l, 32))
                        pe.wait_ge(*small_v.at(l, 3))
                        for i in range(4):
                            ins = mm(ps[:, 4 + i, 0:T], m["wa"][:, i // 2, P * (i % 2):P * (i % 2) + P], m["lrT"][:],
                                     start=True, stop=True)
                        ins.then_inc(z_done.sem, 1)
                    if s == 19:
                        level(-1)
                    if s in range(21, 21 + 2 * LEVELS, 2):
                        level((s - 21) // 2)
                    if s in (35, 37):
                        whole((s - 35) // 2)
                    if s in (28, 30, 32, 34):
                        rotate((s - 28) // 2)
                    if s == 36:
                        prompt_keys()
                    if s in (38, 40):
                        state((s - 38) // 2)
                    if 39 <= s < 43:
                        gla_out(s - 39)
                    if 40 <= s < 44:
                        head_square_sum(s - 40)
                    if s == 43:
                        conv_mean()
                    if s == 45:
                        conv_var()
                    if s in (50, 53, 56):
                        head_square_sum(H + (s - 50) // 3)
                    if 46 <= s:
                        values(s - 46)
                    if 45 <= s < 57:
                        weights_T(s - 45)
                    if 44 <= s < 56:
                        scores(s - 44)

                branch_in = ((m["gla_hi"], m["gla_lo"]), (m["conv_hi"], m["conv_lo"]), (m["diff_hi"], m["diff_lo"]))
                for n in range(N_BR):
                    mc, b = BRANCHES[n]
                    s = BR0 + n
                    split(s)
                    if n == 0:
                        pe.wait_ge(*pair_read[0].at(l, 15))
                        pe.wait_ge(*o_lo.at(l, 1))
                    if n == 1:
                        head_square_sum(2 * H - 1)
                        pe.wait_ge(*pair_read[1].at(l, 14))
                    if n == 2:
                        pe.wait_ge(*ex_a.at(l, 24))
                    if n == 3:
                        pe.wait_ge(*o_lo.at(l, 2))
                    if n == 4:
                        pe.wait_ge(*conv_lo_v.at(l, 1))
                    if n >= 4:
                        pe.wait_ge(*gated.at(l, n - 3))
                    for j in range(4):
                        ins = mix(s, [j * 256, j * 256 + P], [pair[n % 4][:, 0, :], pair[n % 4][:, 1, :]], j, branch_in[b],
                                  j == 0, j == 3)
                    ins.then_inc(piece_used.sem, 1)
                for r in range(N_WO):
                    (cc, half), s = OUT_ORDER[r], WO0 + r
                    split(s)
                    pe.wait_ge(*merged_v.at(l, 2 + 2 * half))
                    if half == 0:
                        if cc < 2:
                            pe.wait_ge(*gated.at(l, 9 + cc))
                        else:
                            pe.wait_ge(*x_ready.at(l, KD + 2 * (cc - 1)))
                    for tiles in (((0, 1),) if half == 0 else ((0,), (1,))):
                        for j in range(4):
                            k = 4 * half + j
                            ins = mix(s, [j * 256 + P * i for i in tiles], [pair[cc % 2][:, i, :] for i in tiles], k, h,
                                      k == 0, k == KD - 1)
                        if tiles == (0,):
                            ins.then_inc(tile_done.sem, 1)
                    ins.then_inc(piece_used.sem, 1)
                    if r == 3:
                        pe.wait_ge(*gated.at(l, N_BR))
                    if r in (3, 5):
                        square_sum(l, 1, r - 3)
                        square_sum(l, 1, r - 2)
                for k in range(4, 8):
                    square_sum(l, 1, k)
                with pe.Fori(0, PAIRS) as i:
                    pe.get_value_cache().nocache = True
                    for half_chunk in range(4):
                        half, part_b = half_chunk % 2, half_chunk // 2
                        s = FI0 + half_chunk
                        pe.wait_ge(hi_ready.sem, l * PIECES + i * 4 + (s + 1 + RAW))
                        pe.wait_ge(lo_ready.sem, l * PIECES + i * 4 + (s + 1 + RAW))
                        if half_chunk == 0:
                            pe.wait_ge(silu_a.sem, l * PAIRS + (i + 1))
                        if half_chunk == 2:
                            pe.wait_ge(u_v.sem, l * PAIRS + (i + 1))
                        for j in range(4):
                            k = 4 * half + j
                            if part_b == 0:
                                pe.wait_ge(*h_lo_ready.at(l, 2 * KD + 2 * (k + 1)))
                            ins = mix(s, [j * 256, j * 256 + P], [pair[part_b][:, 0, :], pair[part_b][:, 1, :]], k, h,
                                      k == 0, k == KD - 1)
                        ins.then_inc(piece_used.sem, 1)
                        if half_chunk == 3:
                            pe.wait_ge(mod_mac.sem, l * mod_mac.per + i * 2 * KD + (mod_mac.credit + 2 * KD))
                            pe.wait_ge(mod_out.sem, l * MOD_CHUNKS + i + mod_out.credit)
                            mod_sums(7, m["acc"][:, 0], True)
                act = (m["act_hi"], m["act_lo"])
                pe.wait_ge(*silu_a.at(l, PAIRS))
                pe.wait_ge(*u_v.at(l, PAIRS))
                for r in range(N_FO):
                    g, kk, s = r // 11, r % 11, FO0 + r
                    split(s)
                    if g == 0:
                        pe.wait_ge(*ulo_v.at(l, kk + 1))
                    if r == 11:
                        pe.wait_ge(*mod_out.at(l, MOD_CHUNKS))
                    for tiles in ((range(4),) if kk < 10 else ([0], [1], [2], [3])):
                        for j in range(2):
                            k = 2 * kk + j
                            ins = mix(s, [j * 512 + P * i for i in tiles], [ps[:, 4 * g + i, 0:T] for i in tiles], k,
                                      act, k == 0, k == KH - 1)
                        if kk == 10 and tiles != [3]:
                            ins.then_inc(tile_done.sem, 1)
                    ins.then_inc(piece_used.sem, 1)
                    if 14 <= r < 18:
                        square_sum(l + 1, 0, r - 14)
                    if r == 5:
                        pe.wait_ge(*mod_mac.at(l, mod_mac.per))
                        pe.wait_ge(*mod_out.at(l, PAIRS))
                        mod_sums(7, m["acc"][:, 0], True)

            for k in range(4, KD):
                square_sum(DEPTH, 0, k)
            for k in range(KD):
                pe.wait_ge(fin_v.sem, k + 1)
                for tt in range(NT):
                    ins = nc.tensor.transpose(ps[:, 2 + 2 * tt + k // 4, P * (k % 4):P * (k % 4) + P],
                                              m["x"][:, k, tt * P:tt * P + P], ident[:])
                if k % 4 == 3:
                    ins.then_inc(fin_p.sem, 1)

        @block.scalar
        def _(act):
            fn = nc.scalar.activation
            act.sem_inc(hi_ready.sem, RAW)
            act.sem_inc(silu_a.sem, 1)
            act.wait_ge(start_p.sem, 1)
            fn(m["csil"][:], ps[:, 7, T:T + 16], ACT.Sigmoid).then_inc(start_a.sem, 1)

            def square(layer, norm, k):
                n = k + 1 if norm else k + 1 - KD
                act.wait_ge(*x_ready.at(layer, KD + n))
                if n - 2 + KD >= 1:
                    act.wait_ge(*sq_used.at(layer, n - 2))
                fn(m["sq"][:, k % 2, :], m["x"][:, k, :], ACT.Square).then_inc(sq_ready.sem, 1)

            for c in range(MOD_CHUNKS + 2):
                if c in (2, 3, 6, 7):
                    square(0, 0, (2, 3, 6, 7).index(c))
                if c < MOD_CHUNKS:
                    w, full = first_mod(c, 0)
                    act.wait_ge(*full)
                    if c == 0:
                        act.wait_ge(start_v.sem, 5)
                    if c >= ACCS:
                        act.wait_ge(mod_red.sem, c - ACCS + 1)
                    for j in range(2):
                        at = KD * j + 1
                        fn(m["acc"][:, c % ACCS, j, :], w[:, 1, :], ACT.Copy, scale=m["csil"][:, at:at + 1]).then_inc(mod_first.sem, 1)
                    w, full = first_mod(c, 1)
                    act.wait_ge(*full)
                    if c >= 2:
                        act.wait_ge(mod_pool.sem, 4 * (c - 1))
                    for k in (2, 3):
                        for j in range(2):
                            at = KD * j + k
                            fn(m["mod_prod"][:, c % 2, k - 2, j, :], w[:, k - 2, :], ACT.Copy,
                               scale=m["csil"][:, at:at + 1]).then_inc(mod_prod.sem, 1)
                if c >= 2:
                    act.wait_ge(mod_red.sem, c - 1)
                    fn(m["mod_sum"][:, 4 * c - 8:4 * c - 4, :], ps[:, 4 + (c - 2) % 4, 0:8]
                       .rearrange("p (a b) -> p a b", b=2), ACT.Copy).then_inc(mod_out.sem, 1)
            act.preload_act_table_set(LN_EXP)
            with act.Fori(0, DEPTH) as l:
                act.get_value_cache().nocache = True

                def high(s):
                    act.wait_ge(*raw_full[s % RAW].at(l, 16 * (s // RAW + 1)))
                    act.wait_ge(*piece_used.at(l, s - SPL + 1))
                    fn(m["w_hi"][:, s % SPL, :], m["w_raw"][:, s % RAW, :], ACT.Copy).then_inc(hi_ready.sem, 1)

                def inverse_rms(which):
                    act.wait_ge(*sq_used.at(l, KD * which))
                    fn(m["rstd"][:], ps[:, 4 * which, 0:T], ACT.Ln, bias=m["eps"][:], scale=1.0 / D).then_inc(rstd_a.sem, 1)
                    act.wait_ge(*rstd_a.at(l, 2 * which + 1))
                    fn(m["rstd"][:], m["rstd"][:], ACT.Exp, scale=-0.5).then_inc(rstd_a.sem, 1)

                def h_high(which, tiles):
                    for k in tiles:
                        act.wait_ge(*t_ready.at(l, 2 * (KD * which + k + 1)))
                        for j, cols in enumerate((slice(0, TP), slice(TP, T))):
                            fn(m["h_hi"][:, k, cols], m["t"][:, k % 2, cols], ACT.Identity,
                               bias=m["mod"][:, 24 * which + k, j:j + 1]).then_inc(h_hi_ready.sem, 1)

                def evacuate(c):
                    col, _ = IN_CHUNKS[c]
                    src, src2 = pair[c % 2], flat[c % 2]
                    if c in (1, 3, 6):
                        return
                    act.wait_ge(*piece_used.at(l, 2 * c + 2))
                    done = pair_read[c % 2].sem
                    if c in (0, 2):
                        if c == 2:
                            act.wait_ge(*pair_read[1].at(l, 1))
                        fn(m["sq"][:], src, ACT.Sigmoid).then_inc(done, 1)
                    elif c in (4, 5):
                        fn(m["gg"][:, 2 * (c - 4):2 * (c - 4) + 2, :], src, ACT.Sigmoid).then_inc(gg_sig.sem, 1)
                    elif c == 7:
                        fn(m["gqk"][:, 0, :, :], src, ACT.Copy, scale=DK ** -0.5).then_inc(done, 1)
                    elif c == 8:
                        fn(m["gqk"][:, 1, :, :], src, ACT.Copy).then_inc(done, 1)
                    elif c in (9, 10, 15, 16):
                        dst, half = (m["gv"], c - 9) if c < 11 else (m["dv"], c - 15)
                        if c == 15:
                            act.wait_ge(*keys_t.at(l, 1))
                        fn(dst[:, :, 256 * half:256 * half + 256], src2[:, 0:NT * 256].rearrange("p (t n) -> p t n", t=NT),
                           ACT.Copy).then_inc(done, 1)
                    elif c < 15:
                        side, ht = (c - 11) // 2, 2 * ((c - 11) % 2)
                        fn(m["dqk"][:, side, ht:ht + 2, :], src, ACT.Copy).then_inc(done, 1)
                    else:
                        i = 2 * (c - 17)
                        if i + 1 >= 15:
                            act.wait_ge(*conv_normed.at(l, 2 * CT))
                        fn(m["gates"][:, i:i + 2, :], src, ACT.Copy).then_inc(done, 1)

                def exp_level(i):
                    act.wait_ge(*built.at(l, 4 * (i + 1) if i < LEVELS else 4 * LEVELS + 2 * (i + 1 - LEVELS)))
                    f = m[f"fac{i % 2}"]
                    fn(f[:], f[:], ACT.Exp, scale=1.0 / 16).then_inc(expd.sem, 1)

                def head_squares(n):
                    if n < H:
                        act.wait_ge(*o_done.at(l, n + 1))
                        if n:
                            act.wait_ge(*o_mul.at(l, 2 * n))
                        fn(m["rstd"][:], ps[:, 4 + n % 2, 0:T], ACT.Square).then_inc(osq.sem, 1)
                    else:
                        act.wait_ge(*pv_done.at(l, 3 * (n - H + 1)))
                        act.wait_ge(*o_lo.at(l, 1))
                        fn(m["gg"][:, n - H, :], ps[:, 7, 0:T], ACT.Copy).then_inc(o_copy.sem, 1)
                        act.wait_ge(*o_copy.at(l, n - H + 1))
                        act.wait_ge(*o_mul.at(l, 2 * H + n - H))
                        fn(m["rstd"][:], m["gg"][:, n - H, :], ACT.Square).then_inc(osq.sem, 1)

                def head_rstd(n):
                    act.wait_ge(*oss.at(l, n + 1))
                    fn(m["rstd"][:], ps[:, 6, 0:T], ACT.Ln, bias=m["eps"][:], scale=1.0 / DV).then_inc(orstd.sem, 1)
                    act.wait_ge(*orstd.at(l, 2 * n + 1))
                    fn(m["rstd"][:], m["rstd"][:], ACT.Exp, scale=-0.5).then_inc(orstd.sem, 1)

                def exp_scores(u):
                    _, q = UNITS[u]
                    act.wait_ge(*mx_v.at(l, 2 * (u + 1)))
                    if u == 0:
                        act.wait_ge(*copied.at(l, 3 * (LEVELS + 1) + 2))
                        act.wait_ge(*etot_a.at(l, 2))
                    else:
                        act.wait_ge(*tp_done.at(l, u))
                    for t in range(2):
                        fn(m["prob"][:, t, 0:keys_of(q)], ps[:, 4 + t, 0:keys_of(q)], ACT.Exp, bias=m["mx"][:, 2 + t:3 + t],
                           scale=DK ** -0.5, accum_out=m["mx"][:, 4 + t:5 + t]).then_inc(ex_a.sem, 1)

                def weights_back(u):
                    _, q = UNITS[u]
                    act.wait_ge(*tp_done.at(l, u + 1))
                    if u >= 2:
                        act.wait_ge(*pv_done.at(l, u - 1))
                    n = keys_of(q) // P
                    fn(m["probT"][:, u % 2, 0:n, :], ps[:, 6, 0:n * P].rearrange("p (t n) -> p t n", t=n),
                       ACT.Copy).then_inc(wt_a.sem, 1)

                flat_t = m["t"][:].rearrange("p a b -> p (a b)")
                for s in range(RAW):
                    high(s)
                for k in range(4, KD):
                    square(l, 0, k)
                inverse_rms(0)
                h_high(0, range(4))
                high(2)
                h_high(0, range(4, KD))
                high(3)
                for s in range(SPL, BR0 + 5):
                    high(s)
                    if (s - 5) % 2 == 0 and 0 <= (s - 5) // 2 < len(IN_CHUNKS):
                        evacuate((s - 5) // 2)
                    if s == 18:
                        act.preload_act_table_set(LN_EXP)
                        act.wait_ge(*setup_v.at(l, 5))
                        fn(m["lam2"][:, 2:4], m["lam2"][:, 0:2], ACT.Exp).then_inc(setup_a.sem, 1)
                    if s == 21:
                        f0 = m["fac0"][:].rearrange("p a b c d -> p (a b c d)")
                        f1 = m["fac1"][:].rearrange("p a b c d -> p (a b c d)")
                        act.wait_ge(*zb.at(l, 4))
                        fn(f0, f1, ACT.Abs).then_inc(za.sem, 1)
                        act.wait_ge(*za.at(l, 1))
                        fn(f0, f0, ACT.Exp, scale=-1.0).then_inc(za.sem, 1)
                        act.wait_ge(*za.at(l, 2))
                        fn(f0, f0, ACT.Ln, bias=m["one"][:]).then_inc(za.sem, 1)
                    if s == 23:
                        act.wait_ge(*scan.at(l, 12))
                        for d in range(2):
                            fn(m["etot"][:, 2 * d:2 * d + 2], m["prefix"][:, d, :, 1 + d, P], ACT.Exp, scale=1.0 / 16
                               ).then_inc(etot_a.sem, 1)
                        exp_level(0)
                    if s == 24:
                        exp_level(1)
                    if s in range(26, 22 + 2 * ROUNDS, 2):
                        exp_level((s - 22) // 2)
                    if s == 40:
                        act.wait_ge(*kT_done.at(l, 1))
                        act.wait_ge(*kv_out.at(l, 0))
                        fn(m["k_rows"][:], ps[:, 7, :], ACT.Copy).then_inc(k_rows.sem, 1)
                    if 44 <= s < 48:
                        head_rstd(s - 44)
                    if 43 <= s < 47:
                        head_squares(s - 43)
                    if s == 48:
                        act.wait_ge(*o_mul.at(l, 2 * H))
                        fn(m["gla_hi"][:], m["gg"][:], ACT.Copy).then_inc(o_hi.sem, 1)
                        for ct in range(CT):
                            act.wait_ge(*centred.at(l, ct + 1))
                            if ct:
                                act.wait_ge(*csq_used.at(l, ct))
                            fn(flat_t[:, 0:AW], m["conv_acc"][:, ct, :], ACT.Square).then_inc(csq.sem, 1)
                    if s == 49:
                        act.wait_ge(*csq_used.at(l, CT))
                        fn(flat_t[:, 0:AW], ps[:, 7, 0:AW], ACT.Ln, bias=m["eps"][:], scale=1.0 / CONV).then_inc(crstd.sem, 1)
                        act.wait_ge(*crstd.at(l, 1))
                        fn(flat_t[:, 0:AW], flat_t[:, 0:AW], ACT.Exp, scale=-0.5).then_inc(crstd.sem, 1)
                    if s in (54, 57, 60, 62):
                        head_rstd(H + (54, 57, 60, 62).index(s))
                    if 49 <= s < 61:
                        weights_back(s - 49)
                    if 48 <= s < 60:
                        exp_scores(s - 48)
                    if s in (52, 55, 58, 61):
                        head_squares(H + (s - 52) // 3)
                act.wait_ge(*o_mul.at(l, 3 * H))
                fn(m["diff_hi"][:], m["gg"][:], ACT.Copy).then_inc(o_hi.sem, 1)
                for ct in range(CT):
                    act.wait_ge(*conv_normed.at(l, 2 * (ct + 1)))
                    fn(m["conv_s"][:, ct, :], m["conv_z"][:, ct, :], ACT.Sigmoid, bias=m["prm"][:, R_LB + ct:R_LB + ct + 1]
                       ).then_inc(conv_sig.sem, 1)
                act.wait_ge(*pair_read[0].at(l, 15))
                act.wait_ge(*pair_read[1].at(l, 14))
                for a, n in ((0, 4), (4, 4), (2 * KD, KD), (KD, KD)):
                    g = m["gates"][:, a:a + n, :]
                    fn(g, g, ACT.Sigmoid).then_inc(gsig.sem, 1)
                    if a == 0:
                        act.wait_ge(*conv_out.at(l, CT))
                        fn(m["conv_hi"][:], m["conv_z"][:], ACT.Copy).then_inc(conv_hi_a.sem, 1)
                    else:
                        high(BR0 + {4: 5, 2 * KD: 6, KD: 7}[a])
                act.preload_act_table_set(LN_EXP)
                for s in range(BR0 + 8, FI0 + 4):
                    high(s)
                    if s in (66, 68, 70, 73):
                        mc = (66, 68, 70, 73).index(s)
                        act.wait_ge(*summed.at(l, 2 * (mc + 1)))
                        fn(m["h_hi"][:, 2 * mc:2 * mc + 2, :], m["gates"][:, 2 * mc:2 * mc + 2, :], ACT.Copy
                           ).then_inc(merged_a.sem, 1)
                    if s in (76, 77, 79, 81):
                        k = 2 * (76, 77, 79, 81).index(s)
                        square(l, 1, k)
                        square(l, 1, k + 1)
                inverse_rms(1)
                h_high(1, range(KD))
                act.preload_act_table_set("silu_and_others")
                with act.Fori(0, PAIRS) as i:
                    act.get_value_cache().nocache = True
                    for j in range(4):
                        s = FI0 + SPL + j
                        act.wait_ge(raw_full[s % RAW].sem, l * raw_full[0].per + i * (16 * 4 // RAW) + 16 * (s // RAW + 1))
                        act.wait_ge(piece_used.sem, l * PIECES + i * 4 + (s + 1))
                        fn(m["w_hi"][:, s % SPL, :], m["w_raw"][:, s % RAW, :], ACT.Copy).then_inc(hi_ready.sem, 1)
                        if j == 1:
                            act.wait_ge(piece_used.sem, l * PIECES + i * 4 + (FI0 + 2 + SPL))
                            act.wait_ge(ulo_v.sem, l * PAIRS + (i + 1))
                            fn(m["sq"][:], pair[0], ACT.Silu).then_inc(silu_a.sem, 1)
                        if j == 3:
                            act.wait_ge(u_v.sem, l * PAIRS + (i + 2))
                            fn(m["act_hi"][:, bass.ds(i * 2, 2), :], m["sq"][:], ACT.Copy).then_inc(uhi_a.sem, 1)
                act.preload_act_table_set(LN_EXP)
                for s in range(FO0 + SPL, PIECES):
                    high(s)
                    if 16 <= s - FO0 < 20:
                        square(l + 1, 0, s - FO0 - 16)

            for k in range(4, KD):
                square(DEPTH, 0, k)
            act.wait_ge(*sq_used.at(DEPTH, 0))
            fn(m["rstd"][:], ps[:, 0, 0:T], ACT.Ln, bias=m["eps"][:], scale=1.0 / D).then_inc(fin_a.sem, 1)
            act.wait_ge(fin_a.sem, 1)
            fn(m["rstd"][:], m["rstd"][:], ACT.Exp, scale=-0.5).then_inc(fin_a.sem, 1)

        @block.vector
        def _(dve):
            v = nc.vector
            for s in (setup_v, u_v, ulo_v):
                dve.sem_inc(s.sem, 1)
            v.memset(m["eps"][:], EPS).then_inc(start_v.sem, 1)
            v.memset(m["one"][:], 1.0).then_inc(start_v.sem, 1)
            v.memset(m["ones"][:], 1.0).then_inc(start_v.sem, 1)
            v.memset(m["wa"][:], 0.0).then_inc(start_v.sem, 1)
            dve.wait_ge(const_in.sem, 64)
            v.tensor_copy(m["masks"][:], m["masks_in"][:]).then_inc(masks_v.sem, 1)
            dve.wait_ge(start_a.sem, 1)
            v.tensor_tensor(m["csil"][:], m["csil"][:], ps[:, 7, T:T + 16], ALU.mult).then_inc(start_v.sem, 1)
            for k in range(KD):
                dve.wait_ge(start_p.sem, k + 2)
                v.tensor_copy(m["x"][:, k, :], ps[:, k, 0:T]).then_inc(x_ready.sem, 1)

            def mod_mac_op(n, k, j, w, acc, before, first=True):
                cond = m["csil"][:, KD * j + k:KD * j + k + 1]
                if n == 0 and first:
                    v.tensor_scalar(acc[:, j, :], w, cond, None, ALU.mult).then_inc(mod_mac.sem, 1)
                else:
                    if n:
                        dve.wait_ge(mod_mac.sem, before + 2 * n + j - 1)
                    v.scalar_tensor_tensor(acc[:, j, :], w, cond, acc[:, j, :], ALU.mult, ALU.add).then_inc(mod_mac.sem, 1)

            dve.wait_ge(start_v.sem, 5)
            for c in range(MOD_CHUNKS):
                for k in range(4, KD):
                    if k % 2 == 0:
                        w, full = first_mod(c, k // 2)
                        dve.wait_ge(*full)
                    for j in range(2):
                        if k == 4:
                            dve.wait_ge(mod_pool.sem, 4 * c + j + 3)
                        mod_mac_op(k - 4, k, j, w[:, k % 2, :], m["acc"][:, c % ACCS], MOD_DVE * c, first=False)

            with dve.Fori(0, DEPTH) as l:
                dve.get_value_cache().nocache = True

                def done(ins, sig, n=None):
                    ins.then_inc(sig.sem, 1)
                    dve.wait_ge(*sig.at(l, n or sig.next()))

                def column(r, n=1):
                    return m["prm"][:, r:r + n]

                def spread(ap, n):
                    return ap.unsqueeze(2).broadcast_to([ap.shape[0], ap.shape[1], n])

                SEGS = ((0, slice(0, TP)), (1, slice(TP, T)))

                def norm_t(which, k):
                    if k >= 2:
                        dve.wait_ge(*h_lo_ready.at(l, 2 * (KD * which + k - 1)))
                    for j, cols in SEGS:
                        done(v.scalar_tensor_tensor(m["t"][:, k % 2, cols], m["x"][:, k, cols], m["eff"][:, which, k, j:j + 1],
                                                    m["rstd"][:, cols], ALU.mult, ALU.mult), t_ready)

                def norm_low(which, k):
                    dve.wait_ge(*h_hi_ready.at(l, 2 * (KD * which + k + 1)))
                    for j, cols in SEGS:
                        v.scalar_tensor_tensor(m["h_lo"][:, k, cols], m["t"][:, k % 2, cols],
                                               m["mod"][:, 24 * which + k, j:j + 1],
                                               m["h_hi"][:, k, cols].bitcast(F32), ALU.add, ALU.subtract
                                               ).then_inc(h_lo_ready.sem, 1)

                def modulated_norm(which):
                    dve.wait_ge(*rstd_a.at(l, 2 * which + 2))
                    norm_t(which, 0)
                    for k in range(1, KD):
                        norm_t(which, k)
                        norm_low(which, k - 1)
                    norm_low(which, KD - 1)

                def add_to_x(tile, src, gate):
                    done(v.scalar_tensor_tensor(m["x"][:, tile, 0:TP], src[:, 0:TP], m["mod"][:, gate + tile, 0:1],
                                                m["x"][:, tile, 0:TP], ALU.mult, ALU.add), x_part)
                    done(v.scalar_tensor_tensor(m["x"][:, tile, TP:T], src[:, TP:T], m["mod"][:, gate + tile, 1:2],
                                                m["x"][:, tile, TP:T], ALU.mult, ALU.add), x_ready,
                         (KD if gate == 16 else 2 * KD) + tile + 1)

                taps_done = [0]

                def taps(n):
                    for i in range(taps_done[0], min(taps_done[0] + n, TAPS * CT)):
                        w, ct = i // CT, i % CT
                        src, acc, wt = m["conv_in"][:, ct, w:w + AW], m["conv_acc"][:, ct, :], m["cw"][:, i:i + 1]
                        if w:
                            dve.wait_ge(*tap.at(l, i - CT + 1))
                            v.scalar_tensor_tensor(acc, src, wt, acc, ALU.mult, ALU.add).then_inc(tap.sem, 1)
                        else:
                            v.tensor_scalar(acc, src, wt, column(R_CB + ct), ALU.mult, ALU.add).then_inc(tap.sem, 1)
                    taps_done[0] = min(taps_done[0] + n, TAPS * CT)

                dve.wait_ge(masks_v.sem, 1)
                dve.wait_ge(*mod_out.at(l, 0))
                dve.wait_ge(*rows_t.at(l, 1))
                done(v.tensor_copy(m["prm"][:], ps[:, 1, 0:R_END]), small_v)
                done(v.tensor_copy(m["cw"][:], ps[:, 1, P:P + TAPS * CT]), small_v)
                done(v.tensor_tensor(m["mod"][:], m["mod_sum"][:], spread(column(R_BMOD, 48), 2), ALU.add), setup_v)
                done(v.scalar_tensor_tensor(m["eff"][:, 0, :, :], m["mod"][:, 8:16, :], 1.0, spread(column(R_N1, 8), 2),
                                            ALU.add, ALU.mult), setup_v)
                done(v.scalar_tensor_tensor(m["eff"][:, 1, :, :], m["mod"][:, 32:40, :], 1.0, spread(column(R_N2, 8), 2),
                                            ALU.add, ALU.mult), setup_v)
                modulated_norm(0)
                for a, b in ((0, PAD), (PAD + TP, Y_S), (Y_S + TS, YW)):
                    done(v.memset(m["conv_in"][:, :, a:b], 0.0), pads)

                for i in range(2):
                    dve.wait_ge(*piece_used.at(l, 4 * i + 4))
                    dve.wait_ge(*pair_read[0].at(l, i + 1))
                    tiles = slice(2 * i, 2 * i + 2)
                    done(v.tensor_tensor(m["conv_in"][:, tiles, Y_P:Y_P + TP], pair[1][:, :, 0:TP], m["sq"][:, :, 0:TP],
                                         ALU.mult), y_prompt_ready)
                    done(v.tensor_tensor(m["conv_in"][:, tiles, Y_S:Y_S + TS], pair[1][:, :, TP:T], m["sq"][:, :, TP:T],
                                         ALU.mult), pair_read[1], i + 1)
                dve.wait_ge(*keys_t.at(l, 1))
                done(v.tensor_copy(m["ckT"][:], ps[:, 6, :].rearrange("p (a b) -> p a b", a=H)), small_v)
                taps(8)
                for i in range(2):
                    dve.wait_ge(*gg_sig.at(l, i + 1))
                    g = m["gg"][:, 2 * i:2 * i + 2, :]
                    done(v.tensor_tensor(g, g, pair[i], ALU.mult), pair_read[i], 3)
                    taps(12)
                dve.wait_ge(*piece_used.at(l, 14))
                done(v.tensor_copy(m["lrT"][:], pair[0][0:2 * RANK, 0, :]), pair_read[0], 4)
                taps(12)
                lam = m["lam"][:].rearrange("p (a b) d -> p a b d", b=2)
                dve.wait_ge(*ctx_in.at(l, 64))
                done(v.tensor_tensor(lam[:, :, 0, :], lam[:, :, 0, :], lam[:, :, 1, :], ALU.mult), setup_v)
                done(v.tensor_reduce(m["lam2"][:, 0:2], lam[:, :, 0, :], AX_X, ALU.add), setup_v)
                taps(12)

                f0, f1 = (m[f][:].rearrange("p a b c d -> p (a b) (c d)") for f in ("fac0", "fac1"))
                dve.wait_ge(*z_done.at(l, 1))
                for i in range(4):
                    done(v.tensor_scalar(f1[:, i, :], ps[:, 4 + i, 0:T], column(R_BA + i), None, ALU.add), zb)
                dve.wait_ge(*setup_a.at(l, 1))
                lam2 = m["lam2"]
                done(v.tensor_tensor(lam2[:, 4:5], lam2[:, 2:3], lam2[:, 3:4], ALU.subtract), setup_v)
                done(v.tensor_scalar(lam2[:, 5:6], lam2[:, 4:5], m["lamc"][:, 0:1], -1.0, ALU.add, ALU.mult), setup_v)
                done(v.tensor_scalar(m["subg"][:], column(R_SUB), m["lamc"][:, 1:2], None, ALU.mult), setup_v)
                dve.wait_ge(*za.at(l, 3))
                done(v.scalar_tensor_tensor(f1, f1, 0.0, f0, ALU.min, ALU.subtract), decay)
                done(v.memset(m["prefix"][:, :, :, :, 0:1], 0.0), decay)
                for n in range(12):
                    d, ht, tt = n // 6, n // 3 % 2, n % 3
                    v.tensor_tensor_scan(m["prefix"][:, d, ht, tt, 1:P + 1], m["ones"][:], m["fac1"][:, d, ht, tt, :], 0.0,
                                         ALU.mult, ALU.add).then_inc(scan.sem, 1)
                dve.wait_ge(*scan.at(l, 12))

                fwd = m["prefix"][:, 0].rearrange("p a b t -> p (a b) t")
                bwd = m["prefix"][:, 1].rearrange("p a b t -> p (a b) t")

                def build(i):
                    f = m[f"fac{i % 2}"]
                    if i >= 2:
                        dve.wait_ge(*level_done.at(l, i))
                        dve.wait_ge(*copied.at(l, 3 * (i - 1)))
                    q, k = (f[:, s].rearrange("p a b t -> p (a b) t") for s in range(2))
                    if i < LEVELS:
                        n, g = 1 << i, 2 * NT

                        def halves(ap):
                            return ap.rearrange("p g (n s j) -> p g n s j", s=2, j=n)

                        def border(ap):
                            return halves(ap[:, :, 0:P])[:, :, :, 1, 0:1].broadcast_to([P, g, P // (2 * n), n])

                        incl, excl = halves(fwd[:, :, 1:P + 1]), halves(bwd[:, :, 0:P])
                        q, k = halves(q), halves(k)
                        v.tensor_tensor(q[:, :, :, 1, :], incl[:, :, :, 1, :], border(fwd), ALU.subtract).then_inc(built.sem, 1)
                        if i >= 2:
                            copy_level(i - 2)
                        v.tensor_tensor(k[:, :, :, 0, :], border(fwd), incl[:, :, :, 0, :], ALU.subtract).then_inc(built.sem, 1)
                        v.tensor_tensor(q[:, :, :, 0, :], border(bwd), excl[:, :, :, 0, :], ALU.subtract).then_inc(built.sem, 1)
                        v.tensor_tensor(k[:, :, :, 1, :], excl[:, :, :, 1, :], border(bwd), ALU.subtract).then_inc(built.sem, 1)
                    elif i == LEVELS:
                        total = fwd[:, :, P:P + 1].broadcast_to([P, 2 * NT, P])
                        v.tensor_copy(q, fwd[:, :, 1:P + 1]).then_inc(built.sem, 1)
                        copy_level(i - 2)
                        v.tensor_tensor(k, total, fwd[:, :, 1:P + 1], ALU.subtract).then_inc(built.sem, 1)
                    else:
                        total = bwd[:, :, P:P + 1].broadcast_to([P, 2 * NT, P])
                        v.tensor_tensor(q, total, bwd[:, :, 0:P], ALU.subtract).then_inc(built.sem, 1)
                        copy_level(i - 2)
                        v.tensor_copy(k, bwd[:, :, 0:P]).then_inc(built.sem, 1)

                def multiply(i):
                    f = m[f"fac{i % 2}"][:].rearrange("p a b c d -> p (a b c d)")
                    if i == 0:
                        dve.wait_ge(*pair_read[1].at(l, 4))
                        dve.wait_ge(*pair_read[0].at(l, 5))
                    dve.wait_ge(*expd.at(l, i + 1))
                    done(v.tensor_tensor(f, f, m["gqk"][:].rearrange("p a b t -> p (a b t)"), ALU.mult), factors)

                def copy_level(i):
                    for tt in range(NT):
                        src, dst = ps[:, 4 + tt, :].rearrange("p (a b) -> p a b", a=H), m["attn"][:, tt]
                        if i < 0:
                            dve.wait_ge(*level_done.at(l, 1))
                            v.tensor_copy(dst, src).then_inc(copied.sem, 1)
                        else:
                            mask = m["masks"][:, i:i + 1, :].broadcast_to([P, H, P])
                            v.copy_predicated(dst, mask, src).then_inc(copied.sem, 1)

                def rope(r):
                    side, ht = r // 2, 2 * (r % 2)
                    rot = ps[:, 7, :].rearrange("p (a b) -> p a b", a=2)
                    x = m["dqk"][:, side, ht:ht + 2, TP:T]
                    cos, sin = (m["rope"][:, i:i + 1, :].broadcast_to([P, 2, TS]) for i in range(2))
                    dve.wait_ge(*rot_done.at(l, r + 1))
                    done(v.tensor_tensor(rot, rot, sin, ALU.mult), roped)
                    done(v.tensor_tensor(x, x, cos, ALU.mult), roped)
                    done(v.tensor_tensor(x, x, rot, ALU.add), roped)

                build(0)
                build(1)
                copy_level(-1)
                multiply(0)
                multiply(1)
                for i in range(2, ROUNDS):
                    build(i)
                    taps(10)
                    multiply(i)
                    if i >= 5:
                        rope(i - 5)
                taps(TAPS * CT)
                def enter(d):
                    f, tt = m[f"fac{(LEVELS + d) % 2}"], 2 - d
                    dve.wait_ge(*etot_a.at(l, 2))
                    for ht in range(2):
                        done(v.tensor_scalar(m["q_enter"][:, d, ht, :], f[:, 0, ht, tt, :],
                                             m["etot"][:, 2 * d + ht:2 * d + ht + 1], None, ALU.mult), entered)

                def crossed(d):
                    dve.wait_ge(*level_done.at(l, LEVELS + 2 + d))
                    done(v.tensor_copy(m["cross"][:, d], ps[:, 4 + d, :].rearrange("p (a b) -> p a b", a=H)), copied)

                def state_keys(d):
                    dve.wait_ge(*st_t.at(l, d + 1))
                    if d:
                        dve.wait_ge(*st_mm.at(l, 1))
                    done(v.tensor_copy(m["stateT"][:], ps[:, 6, 2 * d * P:2 * d * P + 2 * P]
                                       .rearrange("p (a b) -> p a b", a=2)), st_c)

                def state(d):
                    dve.wait_ge(*st_mm.at(l, d + 1))
                    if d:
                        dve.wait_ge(*st_out.at(l, 16))
                    done(v.tensor_copy(m["state_out"][:], ps[0:DK, 7, :].rearrange("p (a b) -> p a b", a=H)), st_v)

                enter(0)
                enter(1)
                crossed(0)
                state_keys(0)
                crossed(1)
                state(0)
                state_keys(1)
                state(1)
                for hh in range(H):
                    dve.wait_ge(*orstd.at(l, 2 * (hh + 1)))
                    done(v.scalar_tensor_tensor(m["rstd"][:], ps[:, 4 + hh % 2, 0:T], column(R_GN), m["rstd"][:], ALU.mult,
                                                ALU.mult), o_mul)
                    g = m["gg"][:, hh, :]
                    done(v.tensor_tensor(g, g, m["rstd"][:], ALU.mult), o_mul)
                dve.wait_ge(*mean_done.at(l, 1))
                for ct in range(CT):
                    a = m["conv_acc"][:, ct, :]
                    done(v.scalar_tensor_tensor(a, ps[:, 7, 0:AW], -1.0 / CONV, a, ALU.mult, ALU.add), centred)
                dve.wait_ge(*o_hi.at(l, 1))
                done(v.tensor_tensor(m["gla_lo"][:], m["gg"][:], m["gla_hi"][:].bitcast(F32), ALU.subtract), o_lo)

                def conv_norm():
                    dve.wait_ge(*crstd.at(l, 2))
                    r = m["t"][:].rearrange("p a b -> p (a b)")
                    for ct in range(CT):
                        for a, b, n in ((0, 0, TP), (A_S, TP, TS)):
                            done(v.scalar_tensor_tensor(m["conv_z"][:, ct, b:b + n], m["conv_acc"][:, ct, a:a + n],
                                                        column(R_LG + ct), r[:, a:a + n], ALU.mult, ALU.mult), conv_normed)

                def attention_gain(hh):
                    dve.wait_ge(*orstd.at(l, 2 * (H + hh + 1)))
                    g = m["gg"][:, hh, :]
                    done(v.scalar_tensor_tensor(g, g, m["subg"][:], m["rstd"][:], ALU.mult, ALU.mult), o_mul)

                mx = m["mx"]
                for u, (hh, q) in enumerate(UNITS):
                    n = keys_of(q)
                    dve.wait_ge(*sc_done.at(l, u + 1))
                    done(v.tensor_reduce(mx[:, 0:2], ps[:, 4:6, 0:n], AX_X, ALU.max), mx_v)
                    done(v.tensor_scalar(mx[:, 2:4], mx[:, 0:2], -DK ** -0.5, None, ALU.mult), mx_v)
                    dve.wait_ge(*ex_a.at(l, 2 * (u + 1)))
                    done(v.reciprocal(mx[:, 6:8], mx[:, 4:6]), w_v)
                    done(v.tensor_scalar(mx[:, 7:8], mx[:, 7:8], lam2[:, 5:6], None, ALU.mult), w_v)
                    p1, p2 = m["prob"][:, 0, 0:n], m["prob"][:, 1, 0:n]
                    done(v.tensor_scalar(p1, p1, mx[:, 6:7], None, ALU.mult), w_v)
                    done(v.scalar_tensor_tensor(p1, p2, mx[:, 7:8], p1, ALU.mult, ALU.add), w_v)
                    if u == 1:
                        conv_norm()
                    if u in (7, 10):
                        attention_gain(u // 3 - 2)
                attention_gain(2)
                attention_gain(3)
                dve.wait_ge(*o_hi.at(l, 2))
                done(v.tensor_tensor(m["diff_lo"][:], m["gg"][:], m["diff_hi"][:].bitcast(F32), ALU.subtract), o_lo)
                for ct in range(CT):
                    dve.wait_ge(*conv_sig.at(l, ct + 1))
                    z = m["conv_z"][:, ct, :]
                    done(v.scalar_tensor_tensor(z, z, column(R_LB + ct), m["conv_s"][:, ct, :], ALU.add, ALU.mult), conv_out)
                for n in range(N_BR):
                    mc, b = BRANCHES[n]
                    g = m["gates"][:, KD * b + 2 * mc:KD * b + 2 * mc + 2, :]
                    dve.wait_ge(*piece_used.at(l, BR0 + n + 1))
                    dve.wait_ge(*gsig.at(l, 1 + mc // 2 if b == 0 else {2: 3, 1: 4}[b]))
                    done(v.tensor_tensor(g, g, pair[n % 4], ALU.mult), gated)
                    if n == 0:
                        dve.wait_ge(*conv_hi_a.at(l, 1))
                        done(v.tensor_tensor(m["conv_lo"][:], m["conv_z"][:], m["conv_hi"][:].bitcast(F32), ALU.subtract),
                             conv_lo_v)
                    if b:
                        a = m["gates"][:, 2 * mc:2 * mc + 2, :]
                        done(v.tensor_tensor(a, a, g, ALU.add), summed)
                    if b == 1:
                        dve.wait_ge(*merged_a.at(l, mc + 1))
                        hi = m["h_hi"][:, 2 * mc:2 * mc + 2, :].bitcast(F32)
                        done(v.tensor_tensor(m["h_lo"][:, 2 * mc:2 * mc + 2, :], a, hi, ALU.subtract), merged_v)
                for cc in range(4):
                    for i in range(2):
                        dve.wait_ge(*(piece_used.at(l, WO0 + OUT_ORDER.index((cc, 1)) + 1) if i else tile_done.at(l, cc + 1)))
                        add_to_x(2 * cc + i, pair[cc % 2][:, i, :], 16)
                modulated_norm(1)

                def mod_chunk(full, before):
                    for k in range(KD):
                        if k % 2 == 0:
                            dve.wait_ge(mod_full[k // 2].sem, full)
                        for j in range(2):
                            mod_mac_op(k, k, j, m["mod_w"][:, k // 2, k % 2, :], m["acc"][:, 0], before)

                def mod_copy(dst):
                    v.tensor_copy(dst, ps[:, 7, 0:8].rearrange("p (a b) -> p a b", b=2)).then_inc(mod_out.sem, 1)

                with dve.Fori(0, PAIRS) as i:
                    dve.get_value_cache().nocache = True
                    mod_chunk(l * mod_full[0].per + i * 16 + (mod_full[0].credit + 16),
                              l * mod_mac.per + i * 2 * KD + mod_mac.credit)
                    dve.wait_ge(silu_a.sem, l * PAIRS + (i + 2))
                    dve.wait_ge(piece_used.sem, l * PIECES + i * 4 + (FI0 + 4 + SPL))
                    v.tensor_tensor(m["sq"][:], m["sq"][:], pair[1], ALU.mult).then_inc(u_v.sem, 1)
                    dve.wait_ge(uhi_a.sem, l * PAIRS + (i + 1))
                    v.tensor_tensor(m["act_lo"][:, bass.ds(i * 2, 2), :], m["sq"][:],
                                    m["act_hi"][:, bass.ds(i * 2, 2), :].bitcast(F32), ALU.subtract).then_inc(ulo_v.sem, 1)
                    dve.wait_ge(mod_red.sem, l * MOD_CHUNKS + i + (mod_red.credit + 1))
                    mod_copy(m["mod_sum"][:, bass.ds(i * 4, 4), :])
                mod_chunk(l * mod_full[0].per + (mod_full[0].credit + 16 * MOD_CHUNKS), l * mod_mac.per
                          + (mod_mac.credit + 2 * KD * PAIRS))
                dve.wait_ge(*mod_red.at(l, MOD_CHUNKS))
                mod_copy(m["mod_sum"][:, 4 * PAIRS:, :])
                for g in range(2):
                    for i in range(4):
                        dve.wait_ge(*(piece_used.at(l, FO0 + 11 * (g + 1)) if i == 3 else tile_done.at(l, 5 + 3 * g + i)))
                        add_to_x(4 * g + i, ps[:, 4 * g + i, 0:T], 40)

            dve.wait_ge(fin_a.sem, 2)
            for k in range(KD):
                v.scalar_tensor_tensor(m["x"][:, k, :], m["x"][:, k, :], m["prm"][:, R_FN + k:R_FN + k + 1], m["rstd"][:],
                                       ALU.mult, ALU.mult).then_inc(fin_v.sem, 1)
            for half in range(2):
                dve.wait_ge(fin_p.sem, half + 1)
                for tt in range(NT):
                    v.tensor_copy(m["stage"][:, tt, 512 * half:512 * half + 512], ps[:, 2 + 2 * tt + half, :]
                                  ).then_inc(fin_v.sem, 1)


_INS = ['x_prompt', 'x_sample', 'cache_diff_k', 'cache_diff_v', 'state_gla', 'c', 'c_ctx', 'w_mod', 'b_mod', 'norm1_g',
        'norm2_g', 'w_in', 'gla_w_a2', 'gla_b_a', 'gla_norm_g', 'conv_w', 'conv_b', 'conv_ln_g', 'conv_ln_b',
        'diff_lambda', 'diff_subln_g', 'w_branch', 'w_out', 'w_ffn_in', 'w_ffn_out', 'final_norm_g']
_OUTS = [((1, TP, D), 'float32'), ((1, TS, D), 'float32'), ((1, DEPTH, TP, H, 2, DK), 'float32'),
         ((1, DEPTH, TP, H, DV), 'float32'), ((1, DEPTH, 2, H, DK, DV), 'float32')]


def _constants():
    import numpy as np
    grid_w, freqs, base = 64, 16, 10000.0
    inv = np.float32(base) ** (-np.arange(freqs, dtype=np.float32) / np.float32(freqs))
    tok = np.arange(TS)
    ang = np.stack([(tok // grid_w).astype(np.float32)[:, None] * inv, (tok % grid_w).astype(np.float32)[:, None] * inv], 1)
    p = np.arange(P)
    a = ang[:, p // 32 % 2, p % 16].T.astype(np.float32)
    rope = np.stack([np.cos(a), np.sin(a)], 1).astype(np.float32)
    swap = np.zeros((P, P), np.float32)
    for i in range(P):
        if i // 16 % 2 == 0:
            swap[i + 16, i] = -1.0
        else:
            swap[i - 16, i] = 1.0
    masks = np.zeros((P, LEVELS, P), np.float32)
    for n in range(LEVELS):
        h = 1 << n
        same = (p[:, None] // (2 * h)) == (p[None, :] // (2 * h))
        masks[:, n, :] = same & ((p[:, None] // h) != (p[None, :] // h))
    lam = np.array([[0.8 - 0.6 * math.exp(-0.3 * n), 1.0 - (0.8 - 0.6 * math.exp(-0.3 * n))] for n in range(DEPTH)],
                   np.float32)
    return {'k_rope': rope, 'k_swap': swap, 'k_ident': np.eye(P, dtype=np.float32), 'k_masks': masks, 'k_lam': lam}


def kernel(**inputs):
    import numpy as _np
    import concourse.bacc as _bacc
    from concourse import mybir as _mybir
    from concourse.bass_utils import run_bass_kernel_spmd as _run

    nc = _bacc.Bacc("TRN2", target_bir_lowering=False, num_devices=1)
    arrays, args = {}, []
    for name, a in [(n, inputs[n]) for n in _INS] + list(_constants().items()):
        a = _np.ascontiguousarray(a)
        arrays[f"in_{name}_dram"] = a
        args.append(nc.dram_tensor(f"in_{name}_dram", a.shape, _mybir.dt.from_np(a.dtype), kind="ExternalInput").ap())
    for i, (shape, dtype) in enumerate(_OUTS):
        dt = _mybir.dt.from_np(_np.dtype(dtype))
        args.append(nc.dram_tensor(f"out_{i}_dram", shape, dt, kind="ExternalOutput").ap())
    program(nc, *args)
    r = _run(nc, [arrays], core_ids=[0])
    return tuple(r.results[0][f"out_{i}_dram"] for i in range(len(_OUTS)))
```
